# Optimizing a Trainium2 kernel written in Bass

```python
import math
import jax, jax.numpy as jnp
from jax import lax
import numpy as np

D_MODEL = 2048
BATCH = 1
SEQ = 256
DEPTH = 2

N_EVEN = (DEPTH + 1) // 2
N_ODD = DEPTH // 2
EPS = 1e-6
ROPE_BASE = 10000.0
S5_WIDTH = 512
S5_GROUP = 16
S5_GROUPS = S5_WIDTH // S5_GROUP
S5_STATE = 64
RET_HEADS = 6
RET_HEAD_DIM = 256
RET_WIDTH = RET_HEADS * RET_HEAD_DIM
RET_CHUNK = 128
EVEN_IN = S5_WIDTH + 4 * RET_WIDTH
MLA_HEADS = 16
MLA_NOPE = 128
MLA_ROPE = 64
MLA_V = 128
MLA_Q_RANK = 512
MLA_KV_RANK = 512
MLA_DOWN = MLA_Q_RANK + MLA_KV_RANK + MLA_ROPE
ATTN_BLOCK = 128
D_FF = 5632
CONV_WIDTH = 3

kernel_name = "hybrid_s5_retention_mla_convffn"

def rms_norm(x, g):
    xf = x.astype(jnp.float32)
    y = xf * lax.rsqrt(jnp.mean(xf * xf, axis=-1, keepdims=True) + EPS)
    return (y * g.astype(jnp.float32)).astype(x.dtype)

def rope_tables(n, dim):
    inv = ROPE_BASE ** (-jnp.arange(0, dim, 2, dtype=jnp.float32) / dim)
    ang = jnp.arange(n, dtype=jnp.float32)[:, None] * inv[None, :]
    return jnp.cos(ang), jnp.sin(ang)

def apply_rope(x, cos, sin):
    x1, x2 = jnp.split(x, 2, axis=-1)
    return jnp.concatenate([x1 * cos - x2 * sin, x2 * cos + x1 * sin], axis=-1).astype(x.dtype)

def _ssm_combine(e1, e2):
    a1r, a1i, b1r, b1i = e1
    a2r, a2i, b2r, b2i = e2
    return (a2r * a1r - a2i * a1i,
            a2r * a1i + a2i * a1r,
            a2r * b1r - a2i * b1i + b2r,
            a2r * b1i + a2i * b1r + b2i)

def s5_mixer(u, lam_re, lam_im, log_dt, b_re, b_im, c_re, c_im, d_skip, glu_w, glu_b):
    f32 = jnp.float32
    bsz, s, _ = u.shape
    lr, li = lam_re.astype(f32), lam_im.astype(f32)
    dt = jnp.exp(log_dt.astype(f32))[:, None]
    mag = jnp.exp(lr * dt)
    ab_re, ab_im = mag * jnp.cos(li * dt), mag * jnp.sin(li * dt)
    den = lr * lr + li * li
    nr, ni = ab_re - 1.0, ab_im
    f_re = (nr * lr + ni * li) / den
    f_im = (ni * lr - nr * li) / den
    br, bi = b_re.astype(f32), b_im.astype(f32)
    bb_re = f_re[..., None] * br - f_im[..., None] * bi
    bb_im = f_re[..., None] * bi + f_im[..., None] * br
    uf = u.astype(f32)
    ug = uf.reshape(bsz, s, S5_GROUPS, S5_GROUP)
    bu_re = jnp.einsum('bsgh,gph->sbgp', ug, bb_re)
    bu_im = jnp.einsum('bsgh,gph->sbgp', ug, bb_im)
    a_re = jnp.broadcast_to(ab_re[None, None], bu_re.shape)
    a_im = jnp.broadcast_to(ab_im[None, None], bu_im.shape)
    _, _, x_re, x_im = lax.associative_scan(_ssm_combine, (a_re, a_im, bu_re, bu_im), axis=0)
    y = (jnp.einsum('sbgp,ghp->bsgh', x_re, c_re.astype(f32))
         - jnp.einsum('sbgp,ghp->bsgh', x_im, c_im.astype(f32)))
    y = y.reshape(bsz, s, S5_WIDTH) + d_skip.astype(f32) * uf
    y = jax.nn.gelu(y)
    y = y * jax.nn.sigmoid(y @ glu_w.astype(f32) + glu_b.astype(f32))
    return y.astype(u.dtype)

def retention(q, k, v, gamma_log):
    bsz, s, h, dk = q.shape
    dv = v.shape[-1]
    c = RET_CHUNK
    n = s // c
    idx = jnp.arange(c, dtype=jnp.float32)
    diff = idx[:, None] - idx[None, :]
    lg = gamma_log[:, None, None]
    dmask = jnp.where(diff[None] >= 0, jnp.exp(jnp.maximum(diff[None], 0.0) * lg), 0.0)
    xi = jnp.exp((idx[None, :] + 1.0) * gamma_log[:, None])
    zeta = jnp.exp((c - 1.0 - idx[None, :]) * gamma_log[:, None])
    g_chunk = jnp.exp(c * gamma_log)

    def to_chunks(t):
        return t.reshape(bsz, n, c, h, t.shape[-1]).transpose(1, 0, 3, 2, 4)

    def step(r, qkv):
        qc, kc, vc = qkv
        inner = jnp.einsum('bhid,bhjd->bhij', qc, kc) * dmask
        o = (jnp.einsum('bhij,bhjd->bhid', inner, vc)
             + jnp.einsum('bhid,bhde->bhie', qc * xi[None, :, :, None], r))
        r = r * g_chunk[None, :, None, None] + jnp.einsum('bhjd,bhje->bhde', kc * zeta[None, :, :, None], vc)
        return r, o

    r0 = jnp.zeros((bsz, h, dk, dv), jnp.float32)
    _, o = lax.scan(step, r0, (to_chunks(q), to_chunks(k), to_chunks(v)))
    return o.transpose(1, 0, 3, 2, 4).reshape(bsz, s, h, dv)

def even_mixer(hn, w_in, lam_re, lam_im, log_dt, b_re, b_im, c_re, c_im, d_skip, glu_w, glu_b,
               ret_norm, w_out, cos, sin, gamma_log):
    bsz, s, _ = hn.shape
    f32 = jnp.float32
    proj = hn @ w_in
    u, q, k, v, g = jnp.split(proj, [S5_WIDTH, S5_WIDTH + RET_WIDTH, S5_WIDTH + 2 * RET_WIDTH,
                                     S5_WIDTH + 3 * RET_WIDTH], axis=-1)
    y_s5 = s5_mixer(u, lam_re, lam_im, log_dt, b_re, b_im, c_re, c_im, d_skip, glu_w, glu_b)
    q = apply_rope(q.astype(f32).reshape(bsz, s, RET_HEADS, RET_HEAD_DIM), cos[:, None], sin[:, None])
    k = apply_rope(k.astype(f32).reshape(bsz, s, RET_HEADS, RET_HEAD_DIM), cos[:, None], sin[:, None])
    k = k * (RET_HEAD_DIM ** -0.5)
    v = v.astype(f32).reshape(bsz, s, RET_HEADS, RET_HEAD_DIM)
    o = retention(q, k, v, gamma_log)
    o = o * lax.rsqrt(jnp.mean(o * o, axis=-1, keepdims=True) + EPS)
    o = o * ret_norm.astype(f32).reshape(RET_HEADS, RET_HEAD_DIM)
    y_ret = (jax.nn.silu(g.astype(f32)) * o.reshape(bsz, s, RET_WIDTH)).astype(hn.dtype)
    return jnp.concatenate([y_s5, y_ret], axis=-1) @ w_out

def mla_mixer(hn, w_down, q_norm, w_uq, kv_norm, w_ukv, w_out, cos, sin):
    bsz, s, _ = hn.shape
    c = hn @ w_down
    cq, ckv, kr = jnp.split(c, [MLA_Q_RANK, MLA_Q_RANK + MLA_KV_RANK], axis=-1)
    q = (rms_norm(cq, q_norm) @ w_uq).reshape(bsz, s, MLA_HEADS, MLA_NOPE + MLA_ROPE)
    qn = q[..., :MLA_NOPE]
    qr = apply_rope(q[..., MLA_NOPE:], cos[:, None], sin[:, None])
    kr = apply_rope(kr, cos, sin)
    kv = (rms_norm(ckv, kv_norm) @ w_ukv).reshape(bsz, s, MLA_HEADS, MLA_NOPE + MLA_V)
    kn, v = kv[..., :MLA_NOPE], kv[..., MLA_NOPE:]
    scale = (MLA_NOPE + MLA_ROPE) ** -0.5
    outs = []
    for blk in range(s // ATTN_BLOCK):
        s0, s1 = blk * ATTN_BLOCK, (blk + 1) * ATTN_BLOCK
        sc = (jnp.einsum('bqhd,bkhd->bhqk', qn[:, s0:s1], kn[:, :s1])
              + jnp.einsum('bqhr,bkr->bhqk', qr[:, s0:s1], kr[:, :s1])).astype(jnp.float32) * scale
        mask = jnp.arange(s0, s1)[:, None] >= jnp.arange(s1)[None, :]
        sc = jnp.where(mask, sc, -1e30)
        p = jax.nn.softmax(sc, axis=-1).astype(v.dtype)
        outs.append(jnp.einsum('bhqk,bkhd->bqhd', p, v[:, :s1]))
    o = jnp.concatenate(outs, axis=1).reshape(bsz, s, MLA_HEADS * MLA_V)
    return o @ w_out

def conv_ffn(hn, w_up, conv_w, conv_b, w_down):
    a = hn @ w_up
    ap = jnp.pad(a, ((0, 0), (CONV_WIDTH - 1, 0), (0, 0)))
    a = ap[:, :-2] * conv_w[0] + ap[:, 1:-1] * conv_w[1] + ap[:, 2:] * conv_w[2] + conv_b
    gate, val = jnp.split(a, 2, axis=-1)
    return (jax.nn.silu(gate) * val) @ w_down

def setup_inputs(seed: int = 0) -> dict:
    key = jax.random.key(seed)
    ks = jax.random.split(key, 32)
    f32 = jnp.float32

    def nrm(k, shape, std):
        return std * jax.random.normal(k, shape, f32)

    E, O, L = N_EVEN, N_ODD, DEPTH
    G, P, H = S5_GROUPS, S5_STATE, S5_GROUP
    lam_im = jnp.broadcast_to(jnp.pi * jnp.arange(P, dtype=f32), (E, G, P))
    return {
        "x": nrm(ks[0], (BATCH, SEQ, D_MODEL), 1.0),
        "ln_mix_even": 1.0 + nrm(ks[1], (E, D_MODEL), 0.02),
        "w_in_even": nrm(ks[2], (E, D_MODEL, EVEN_IN), D_MODEL ** -0.5),
        "s5_lambda_re": -0.5 + nrm(ks[3], (E, G, P), 0.01),
        "s5_lambda_im": lam_im + 0.0,
        "s5_log_dt": jax.random.uniform(ks[4], (E, G), f32, math.log(1e-3), math.log(1e-1)),
        "s5_b_re": nrm(ks[5], (E, G, P, H), (1.0 / math.sqrt(H)) / math.sqrt(2.0)),
        "s5_b_im": nrm(ks[6], (E, G, P, H), (1.0 / math.sqrt(H)) / math.sqrt(2.0)),
        "s5_c_re": nrm(ks[7], (E, G, H, P), (1.0 / math.sqrt(P)) / math.sqrt(2.0)),
        "s5_c_im": nrm(ks[8], (E, G, H, P), (1.0 / math.sqrt(P)) / math.sqrt(2.0)),
        "s5_d": nrm(ks[9], (E, S5_WIDTH), 1.0),
        "s5_glu_w": nrm(ks[10], (E, S5_WIDTH, S5_WIDTH), S5_WIDTH ** -0.5),
        "s5_glu_b": nrm(ks[11], (E, S5_WIDTH), 0.01),
        "ret_norm": 1.0 + nrm(ks[12], (E, RET_WIDTH), 0.02),
        "w_out_even": nrm(ks[13], (E, D_MODEL, D_MODEL), D_MODEL ** -0.5),
        "ln_mix_odd": 1.0 + nrm(ks[14], (O, D_MODEL), 0.02),
        "mla_w_down": nrm(ks[15], (O, D_MODEL, MLA_DOWN), D_MODEL ** -0.5),
        "mla_q_norm": 1.0 + nrm(ks[16], (O, MLA_Q_RANK), 0.02),
        "mla_w_uq": nrm(ks[17], (O, MLA_Q_RANK, MLA_HEADS * (MLA_NOPE + MLA_ROPE)), MLA_Q_RANK ** -0.5),
        "mla_kv_norm": 1.0 + nrm(ks[18], (O, MLA_KV_RANK), 0.02),
        "mla_w_ukv": nrm(ks[19], (O, MLA_KV_RANK, MLA_HEADS * (MLA_NOPE + MLA_V)), MLA_KV_RANK ** -0.5),
        "w_out_odd": nrm(ks[20], (O, MLA_HEADS * MLA_V, D_MODEL), (MLA_HEADS * MLA_V) ** -0.5),
        "ln_ffn": 1.0 + nrm(ks[21], (L, D_MODEL), 0.02),
        "ffn_w_up": nrm(ks[22], (L, D_MODEL, 2 * D_FF), D_MODEL ** -0.5),
        "ffn_conv_w": nrm(ks[23], (L, CONV_WIDTH, 2 * D_FF), CONV_WIDTH ** -0.5),
        "ffn_conv_b": nrm(ks[24], (L, 2 * D_FF), 0.01),
        "ffn_w_down": nrm(ks[25], (L, D_FF, D_MODEL), D_FF ** -0.5),
        "ln_final": 1.0 + nrm(ks[26], (D_MODEL,), 0.02),
    }

def reference(x, ln_mix_even, w_in_even, s5_lambda_re, s5_lambda_im, s5_log_dt, s5_b_re, s5_b_im,
              s5_c_re, s5_c_im, s5_d, s5_glu_w, s5_glu_b, ret_norm, w_out_even, ln_mix_odd,
              mla_w_down, mla_q_norm, mla_w_uq, mla_kv_norm, mla_w_ukv, w_out_odd, ln_ffn,
              ffn_w_up, ffn_conv_w, ffn_conv_b, ffn_w_down, ln_final):
    s = x.shape[1]
    ret_cos, ret_sin = rope_tables(s, RET_HEAD_DIM)
    mla_cos, mla_sin = rope_tables(s, MLA_ROPE)
    gamma_log = jnp.log(1.0 - 2.0 ** (-5.0 - jnp.arange(RET_HEADS, dtype=jnp.float32)))
    h = x
    for layer in range(DEPTH):
        i = layer // 2
        if layer % 2 == 0:
            h = h + even_mixer(rms_norm(h, ln_mix_even[i]), w_in_even[i], s5_lambda_re[i], s5_lambda_im[i],
                               s5_log_dt[i], s5_b_re[i], s5_b_im[i], s5_c_re[i], s5_c_im[i], s5_d[i],
                               s5_glu_w[i], s5_glu_b[i], ret_norm[i], w_out_even[i],
                               ret_cos, ret_sin, gamma_log)
        else:
            h = h + mla_mixer(rms_norm(h, ln_mix_odd[i]), mla_w_down[i], mla_q_norm[i], mla_w_uq[i],
                              mla_kv_norm[i], mla_w_ukv[i], w_out_odd[i], mla_cos, mla_sin)
        h = h + conv_ffn(rms_norm(h, ln_ffn[layer]), ffn_w_up[layer], ffn_conv_w[layer],
                         ffn_conv_b[layer], ffn_w_down[layer])
    return rms_norm(h, ln_final)


_drawn_inputs = setup_inputs


def setup_inputs(seed=0):
    import zlib

    import numpy as np

    out = dict(_drawn_inputs(seed))
    spreads = {}
    factors = {'s5_lambda_re': 64.0,
     's5_lambda_im': 43.856,
     's5_log_dt': 44.336,
     's5_b_re': 62.912,
     's5_b_im': 61.504,
     's5_c_re': 61.64,
     's5_c_im': 61.688,
     's5_glu_b': 8.0,
     'ret_norm': 5.074,
     'ln_mix_odd': 8.0,
     'mla_q_norm': 8.0,
     'mla_kv_norm': 8.0,
     'ln_ffn': 2.873,
     'ffn_conv_b': 5.871,
     'ln_final': 8.421}
    for name, (base, spread) in spreads.items():
        noise = np.random.default_rng([zlib.crc32(name.encode()), seed]).standard_normal(out[name].shape)
        drawn = base * np.exp(spread * noise) if base else spread * noise
        out[name] = __import__('jax').numpy.asarray(drawn.astype(out[name].dtype))
    for name, factor in factors.items():
        out[name] = (out[name] * factor).astype(out[name].dtype)
    return out
```

```python
import math
from contextlib import ExitStack

import numpy as np
import concourse.bass as bass
from concourse import mybir

P = 128
T = 256
D = 2048
KD = D // P
S5W, S5G, S5H, S5P = 512, 32, 16, 64
RH, RD = 6, 256
MH, MN, MR, MV = 16, 128, 64, 128
RANK = 512
KR = RANK // P
DFF = 5632
FS = DFF // 256
GS = FS // 2
GK = 2 * GS
EPS = 1e-6
SLOTS = 4

VEC = {}
_c = 0
for _n, _w in (("g_even", KD), ("g_odd", KD), ("g_ffn", 2 * KD), ("g_fin", KD), ("ret", 2 * RH), ("d", KR),
               ("glub", KR), ("qn", KR), ("kvn", KR), ("lre", KD), ("lim", KD), ("ldt", KD)):
    VEC[_n] = _c
    _c += _w
NVEC = _c

IN_P0, IN_E0 = 0, 0
OE_P0, OE_E0 = IN_P0 + 104, IN_E0 + 26
UPP, DNP = 8 * GS, 8 * 8
F0_P0, F0_E0 = OE_P0 + 32, OE_E0 + 8
MD_P0, MD_E0 = F0_P0 + 2 * (UPP + DNP), F0_E0 + 2 * (2 * GS + 8)
MP_P0 = MD_P0 + 18
OO_P0, OO_E0 = MP_P0 + 32, MD_E0 + 5
F1_P0, F1_E0 = OO_P0 + 32, OO_E0 + 8
F0_L0, MD_L0, F1_L0 = 26, 26 + 4 * GS, 31 + 4 * GS
END_P = F1_P0 + 2 * (UPP + DNP)


def at(c, s=0, r=None):
    return c if r is None else r * s + c


def build(nc, A, out):
    fp32, f32r, i32 = mybir.dt.float32, mybir.dt.float32r, mybir.dt.int32
    ALU, ACT, AX = mybir.AluOpType, mybir.ActivationFunctionType, mybir.AxisListType
    ds = bass.ds
    f = lambda ap: ap.bitcast(fp32)

    ctx = ExitStack()
    with ctx:
        def sb(name, shape, dt=fp32, c=ctx):
            return c.enter_context(nc.sbuf_tensor(name, shape, dt))

        def sem(name):
            return ctx.enter_context(nc.semaphore(name))

        H = sb("H", [P, KD, T])
        XS = sb("XS", [P, KD, 2 * T], f32r)
        raw = sb("raw", [P, SLOTS, 2048])
        hi = sb("hi", [P, SLOTS, 1024], f32r)
        lo = sb("lo", [P, SLOTS, 1024], f32r)
        vec = sb("vec", [P, NVEC])
        ident = sb("ident", [P, P])
        ones = sb("ones", [P, P])
        acc = sb("acc", [P, 2, T])
        rn = sb("rn", [P, T])
        lot = sb("lot", [P, 2, T])
        txn = sb("txn", [P, 2, 2, T])
        sq = sb("sq", [P, 2, T])
        rtok = sb("rtok", [P, 2])
        mark = sb("mark", [P, 1])
        nwt = sb("nwt", [P, 3, T])

        even = ExitStack()
        YE = sb("YE", [P, 12, 2 * T], f32r, even)
        s5o = ExitStack()
        E = sb("E", [P, 2, 2, 2, T], fp32, s5o)
        s5o.close()
        Y5 = sb("Y5", [P, KR, 2 * T], f32r, even)
        cosR = sb("cosR", [P, T], fp32, even)
        sinR = sb("sinR", [P, T], fp32, even)
        dec = sb("dec", [P, T], fp32, even)
        KRo = sb("KRo", [P, 2, T], fp32, even)
        QRo = sb("QRo", [P, 2, T], fp32, even)
        Vr = sb("Vr", [P, 2, T], fp32, even)
        Gr = sb("Gr", [P, 2, T], fp32, even)
        Pm = sb("Pm", [P, T + P], fp32, even)
        kq = sb("kq", [P, 2, T], fp32, even)
        S = sb("S", [P, 3, 2, 2, T], fp32, even)
        sB, sT1, sT2 = S[:, 0], S[:, 1], S[:, 2]
        gluw = S[:, :, :, :, :].rearrange("p a b c t -> p (a b c t)")[:, 0:KR * S5W]\
            .rearrange("p (k n) -> p k n", k=KR)
        g1 = sb("g1", [P, 2, 2, T // 2], fp32, even)
        g2 = sb("g2", [P, 2, 2, T // 2], fp32, even)
        U = sb("U", [P, KR, T], fp32, even)
        BT = sb("BT", [P, KR, 2, P], fp32, even)
        Bst = sb("Bst", [P, 2, P], fp32, even)
        Cst = sb("Cst", [P, 4, 2, 32], fp32, even)
        Ust = sb("Ust", [P, T], fp32, even)
        ph = sb("ph", [P, 8, 2, KD], fp32, even)
        mag = sb("mag", [P, KD], fp32, even)
        minus = sb("minus", [P, 1], fp32, even)
        phst = sb("phst", [P, 8, 2, 2], fp32, even)
        magst = sb("magst", [P, 2], fp32, even)
        even.close()
        Ef = E[:, 1].rearrange("p a b t -> p (a b t)")
        pt = Ef[:, 0:32 * KD].rearrange("p (n c) -> p n c", c=KD)
        pti = Ef[:, 32 * KD:33 * KD].bitcast(i32)
        sigs = sT2.rearrange("p a b t -> p (a b) t")

        odd = ExitStack()
        YO = sb("YO", [P, KD, 2 * T], f32r, odd)
        CS = sb("CS", [P, 2 * KR, 2 * T], f32r, odd)
        C8 = sb("C8", [P, 8, T], fp32, odd)
        caus = sb("caus", [P, 3 * P], fp32, odd)
        mcos = sb("mcos", [P, T], fp32, odd)
        msin = sb("msin", [P, T], fp32, odd)
        swp = sb("swp", [P, P], fp32, odd)
        QN = sb("QN", [P, 2, T], fp32, odd)
        KN = sb("KN", [P, 2, T], fp32, odd)
        QX = sb("QX", [P, T], fp32, odd)
        QRp = sb("QRp", [P, T], fp32, odd)
        KX = sb("KX", [P, T], fp32, odd)
        KRp = sb("KRp", [P, T], fp32, odd)
        rt = sb("rt", [P, 2, T], fp32, odd)
        lo4 = sb("lo4", [P, 5, T], fp32, odd)
        st8 = sb("st8", [P, 2, 6], fp32, odd)
        rc = sb("rc", [P, T], fp32, odd)
        cn = sb("cn", [P, 2, 2, T], fp32, odd)
        odd.close()
        Cf = C8[:, :, :].rearrange("p k t -> p (k t)")
        Sc = Cf[:, 0:6 * P].rearrange("p (h n) -> p h n", h=2)
        PT = Cf[:, 6 * P:12 * P].rearrange("p (h n) -> p h n", h=2)
        V2 = Cf[:, 12 * P:16 * P].rearrange("p (h n) -> p h n", h=2)

        ffn = ExitStack()
        YF = sb("YF", [P, GK, 2 * T], f32r, ffn)
        apad = sb("apad", [P, 2, 2, T + 2], fp32, ffn)
        cvo = sb("cvo", [P, 2, 2, T], fp32, ffn)
        sg = sb("sg", [P, 2, T], fp32, ffn)
        hid = sb("hid", [P, 2, T], fp32, ffn)
        cw = sb("cw", [P, FS, 16], fp32, ffn)
        cws = sb("cws", [P, 16], fp32, ffn)
        ctmp = sb("ctmp", [P, 2, 2, T], fp32, ffn)
        ffn.close()

        PS = ctx.enter_context(nc.psum_tensor("PS", [P, 8, 512], fp32))

        raw_full = [sem(f"raw_full{i}") for i in range(SLOTS)]
        hi_ready = sem("hi_ready")
        lo_ready = sem("lo_ready")
        piece_done = sem("piece_done")
        lo_copied = sem("lo_copied")
        bank_free = sem("bank_free")
        x_in = [sem(f"x_in{i}") for i in range(4)]
        small_in = sem("small_in")
        ones_set = sem("ones_set")
        sq_ready = sem("sq_ready")
        sq_added = sem("sq_added")
        ssq_ready = sem("ssq_ready")
        sum_done = sem("sum_done")
        var_ready = sem("var_ready")
        sd_ready = sem("sd_ready")
        rn_ready = sem("rn_ready")
        rt_done = sem("rt_done")
        rt_ready = sem("rt_ready")
        a_ready = sem("a_ready")
        xt_ready = sem("xt_ready")
        xh_ready = sem("xh_ready")
        xl_ready = sem("xl_ready")

        block = ctx.enter_context(nc.Block())
        pair = lambda e: 2 * ((e + (e >= OO_E0)) % 2)

        @block.sync
        def _(sp):
            def load(u, s, r, src, n):
                if u >= SLOTS:
                    sp.wait_ge(lo_ready, at(2 * (u - SLOTS) + 2, 2 * s, r))
                sp.dma_start(raw[:, u % SLOTS, 0:n], src).then_inc(raw_full[u % SLOTS], 16)

            def stream(name, p0, units, n, base=0):
                u0, w = p0 // 2, A[name]
                turns = units // 4
                with sp.Fori(0, turns) as r:
                    for i in range(4):
                        load(u0 + i, 4, r, w[ds(r * 4 + (base + i), 1), :, :].rearrange("a p n -> p (a n)"), n)
                for i in range(4 * turns, units):
                    load(u0 + i, 0, None, w[base + i, :, :], n)

            def feed_forward(layer, p0):
                for half in range(2):
                    p = p0 + half * (UPP + DNP)
                    stream("ffn_up", p, 4 * GS, 2048, (2 * layer + half) * 4 * GS)
                    stream("ffn_dn", p + UPP, 32, 11 * P, (2 * layer + half) * 32)

            for kind, i in ("x0", "w0", "x1", "x2", "w1", "x3", "w2", "w3"):
                i = int(i)
                if kind == "x":
                    sp.dma_start(H[:, 4 * i:4 * i + 4, :], A["x"][:, 4 * i:4 * i + 4, :]).then_inc(x_in[i], 16)
                else:
                    load(i, 0, None, A["w_in"][i, :, :], 2048)
            with sp.Fori(0, 12) as r:
                for i in range(4):
                    load(4 + i, 4, r, A["w_in"][ds(r * 4 + (4 + i), 1), :, :].rearrange("a p n -> p (a n)"), 2048)
            stream("w_oe", OE_P0, 16, 2048)
            feed_forward(0, F0_P0)
            stream("mla_dn", MD_P0, 9, 2048)
            u0 = MP_P0 // 2
            with sp.Fori(0, 4) as r:
                for i in range(2):
                    load(u0 + 2 * i, 4, r, A["w_uq"][ds(r * 2 + i, 1), :, :].rearrange("a p n -> p (a n)"), 1536)
                    load(u0 + 2 * i + 1, 4, r,
                         A["w_ukv"][ds(r * 2 + i, 1), :, :].rearrange("a p n -> p (a n)"), 2048)
            stream("w_oo", OO_P0, 16, 2048)
            feed_forward(1, F1_P0)

        def geometry(kind, p):
            if kind == "std":
                return 1024 * (p % 2), 1024
            if kind == "down":
                return 768 * (p % 2), (768, 640)[p % 2]
            if kind == "uq":
                return 768 * (p % 2), 768
            raise ValueError(kind)

        even_loads = sem("even_loads")
        bb_ready = sem("bb_ready")
        u_ready = sem("u_ready")
        c_ready = sem("c_ready")
        kx_ready = sem("kx_ready")
        bt_psum = sem("bt_psum")
        bt_ready = sem("bt_ready")
        kq_ready = sem("kq_ready")
        v_ready = sem("v_ready")
        s_done = sem("s_done")
        pm_ready = sem("pm_ready")
        o_done = sem("o_done")
        osq_ready = sem("osq_ready")
        osum_done = sem("osum_done")
        ovar_ready = sem("ovar_ready")
        osd_ready = sem("osd_ready")
        gs_ready = sem("gs_ready")
        yt_ready = sem("yt_ready")
        yh_ready = sem("yh_ready")
        yl_ready = sem("yl_ready")
        dec_in = sem("dec_in")
        cst_in = sem("cst_in")
        staged = sem("staged")
        cneg_ready = sem("cneg_ready")
        ku_ready = sem("ku_ready")
        den_ready = sem("den_ready")
        bu_done = sem("bu_done")
        bu_copied = sem("bu_copied")
        w_ready = sem("w_ready")
        z_ready = sem("z_ready")
        c_done = sem("c_done")
        y5_ready = sem("y5_ready")
        ge_ready = sem("ge_ready")
        gluw_in = sem("gluw_in")
        glu_done = sem("glu_done")
        glu_sig = sem("glu_sig")
        glu_mul = sem("glu_mul")
        glu_hi = sem("glu_hi")
        glu_lo = sem("glu_lo")

        conv_in = sem("conv_in")
        cws_ready = sem("cws_ready")
        cv_ready = sem("cv_ready")
        vc_ready = sem("vc_ready")
        silu_ready = sem("silu_ready")
        hid_ready = sem("hid_ready")
        hh_ready = sem("hh_ready")
        hl_ready = sem("hl_ready")

        odd_loads = sem("odd_loads")
        csq_ready = sem("csq_ready")
        csum_done = sem("csum_done")
        cvar_ready = sem("cvar_ready")
        csd_ready = sem("csd_ready")
        ct_ready = sem("ct_ready")
        ch_ready = sem("ch_ready")
        cl_ready = sem("cl_ready")
        sw_done = sem("sw_done")
        qa_copied = sem("qa_copied")
        qa_free = sem("qa_free")
        kb_copied = sem("kb_copied")
        kb_free = sem("kb_free")
        v2_ready = sem("v2_ready")
        kr_ready = sem("kr_ready")
        kx_copied = sem("kx_copied")
        qr_ready = sem("qr_ready")
        sc_done = sem("sc_done")
        sc_read = sem("sc_read")
        mx_ready = sem("mx_ready")
        ex_ready = sem("ex_ready")
        pn_ready = sem("pn_ready")
        pt_done = sem("pt_done")
        pt_ready = sem("pt_ready")
        at_done = sem("at_done")
        ah_ready = sem("ah_ready")
        al_ready = sem("al_ready")
        fin_ready = sem("fin_ready")
        stored = sem("stored")

        @block.scalar
        def _(act):
            def split(p, s, r, kind="std"):
                u = p // 2
                off, n = geometry(kind, p)
                act.wait_ge(raw_full[u % SLOTS], at(16 * (u // SLOTS + 1), 2 * s, r))
                if p >= SLOTS:
                    act.wait_ge(piece_done, at(p - SLOTS + 1, s, r))
                act.activation(hi[:, p % SLOTS, 0:n], raw[:, u % SLOTS, off:off + n], ACT.Copy).then_inc(hi_ready, 1)

            def splits(p, s=0, r=None, kinds=("std",) * 4):
                for i, k in enumerate(kinds):
                    split(p + i, s, r, k)

            def copy_low(p_end, e, sp_=0, se=0, r=None):
                act.wait_ge(piece_done, at(p_end, sp_, r))
                if e > 0:
                    act.wait_ge(bank_free, at(e, se, r))
                b = pair(e)
                act.activation(lot[:, :, :], PS[:, b:b + 2, T:2 * T], ACT.Copy).then_inc(lo_copied, 1)

            def square_quarter(c):
                act.wait_ge(x_in[c], 16)
                if c >= 2:
                    act.wait_ge(sq_added, c - 1)
                act.activation((sT1, sT2)[c % 2].rearrange("p a b t -> p (a b) t"), H[:, 4 * c:4 * c + 4, :],
                               ACT.Square).then_inc(sq_ready, 1)

            def round_x(n, j, s=0, r=None):
                act.wait_ge(xt_ready, at(8 * n + j + 1, s, r))
                x = XS[:, 2 * j:2 * j + 2, :] if r is None else XS[:, ds(r * (2 * s) + 2 * j, 2), :]
                act.activation(x[:, :, 0:T], txn[:, j % 2, :, :], ACT.Copy).then_inc(xh_ready, 1)

            def root(n):
                act.wait_ge(var_ready, n + 1)
                act.activation(nwt[:, 1, :], nwt[:, 0, :], ACT.Sqrt).then_inc(sd_ready, 1)

            def first_step(n, p):
                splits(p, kinds=("std",) * 2)
                root(n)
                splits(p + 2, kinds=("std",) * 2)

            act.dma_start(vec[:, :], A["vec"]).then_inc(small_in, 16)
            act.dma_start(ident[:, :], A["ident"]).then_inc(small_in, 16)
            act.dma_start(cosR[:, :], A["cosR"]).then_inc(even_loads, 16)
            act.dma_start(sinR[:, :], A["sinR"]).then_inc(even_loads, 16)
            act.dma_start(sB[:, :, :, :].rearrange("p a b t -> p (a b t)"), A["s5b"]).then_inc(even_loads, 16)
            for c in range(4):
                square_quarter(c)
                round_x(0, 2 * c)
                split(c, 0, None)
                round_x(0, 2 * c + 1)

            first_step(0, 4)
            copy_low(4, 0)
            splits(8)
            copy_low(8, 1)
            act.wait_ge(rt_done, 1)
            act.activation(rtok[:, :], PS[:, 7, T:T + 2], ACT.Copy).then_inc(rt_ready, 1)

            def even_head(r, h0, s5, glu=False):
                p0, e0 = 8 + 16 * h0, 2 + 4 * h0
                H_ = lambda c, s: at(c + s * h0, s, r)
                S_ = lambda c, s: at(c + s * (h0 - 1), s, r)

                def bu_copy(m):
                    act.wait_ge(bu_done, S_(m + 1, 4))
                    if m % 2 == 0 and h0 - 1 + m > 0:
                        act.wait_ge(z_ready, S_(m // 2, 2))
                    act.activation(sB[:, :, m % 2, :], PS[:, 7, :].rearrange("p (a t) -> p a t", a=2),
                                   ACT.Copy).then_inc(bu_copied, 1)
                if h0:
                    act.wait_ge(pm_ready, H_(0, 1))
                act.dma_start(dec[:, :], A["dec"][h0, :, :] if r is None else
                              A["dec"][ds(r + h0, 1), :, :].rearrange("a p n -> p (a n)")).then_inc(dec_in, 16)
                if s5:
                    if h0 > 1:
                        act.wait_ge(c_done, S_(0, 2))
                    act.dma_start(Cst[:, :, :, :].rearrange("p a b c -> p (a b c)"),
                                  A["s5c"][h0 - 1, :, :] if r is None else
                                  A["s5c"][ds(r + (h0 - 1), 1), :, :].rearrange("a p n -> p (a n)")).then_inc(cst_in, 16)
                if glu:
                    act.wait_ge(c_done, 8)
                    act.dma_start(gluw, A["gluw"]).then_inc(gluw_in, 16)
                    act.wait_ge(y5_ready, 4)
                    act.activation(U[:, :, :], U[:, :, :], ACT.Gelu_apprx_tanh).then_inc(ge_ready, 1)
                for i in range(4):
                    split(p0 + 4 + i, 16, r)
                    if s5 and i < 2:
                        bu_copy(i)
                copy_low(p0 + 4, e0, 16, 4, r)
                splits(p0 + 8, 16, r)
                copy_low(p0 + 8, e0 + 1, 16, 4, r)
                for i in range(4):
                    split(p0 + 12 + i, 16, r)
                    if s5 and i in (1, 2):
                        bu_copy(i + 1)
                act.wait_ge(piece_done, at(p0 + 12, 16, r))
                act.wait_ge(bank_free, at(e0 + 2, 4, r))
                act.activation(Vr[:, 0, :], PS[:, pair(e0 + 2), 0:T], ACT.Copy, scale=rtok[:, 0:1]).then_inc(lo_copied, 1)
                if glu:
                    act.wait_ge(small_in, 32)
                    act.wait_ge(glu_done, 4)
                    for t in range(KR):
                        ins = act.activation(sigs[:, t, :], PS[:, 6 + t // 2, (t % 2) * T:(t % 2 + 1) * T], ACT.Sigmoid,
                                             bias=vec[:, VEC["glub"] + t:VEC["glub"] + t + 1])
                    ins.then_inc(glu_sig, 1)
                act.wait_ge(o_done, H_(1, 1))
                act.activation(sq[:, :, :], PS[:, 5, :].rearrange("p (a t) -> p a t", a=2), ACT.Square).then_inc(osq_ready, 1)
                splits(p0 + 16, 16, r)
                if h0 == 0:
                    act.wait_ge(bt_psum, 8)
                    for i in range(2):
                        act.activation(BT[:, 2 * i:2 * i + 2, :, :].rearrange("p a b c -> p (a b c)"), PS[:, 6 + i, :],
                                       ACT.Copy).then_inc(bt_ready, 1)
                if glu:
                    act.wait_ge(glu_mul, 1)
                    act.activation(Y5[:, :, 0:T], sigs, ACT.Copy).then_inc(glu_hi, 1)
                copy_low(p0 + 16, e0 + 3, 16, 4, r)
                act.wait_ge(ovar_ready, H_(1, 1))
                act.activation(nwt[:, 1, :], nwt[:, 0, :], ACT.Sqrt).then_inc(osd_ready, 1)
                act.wait_ge(ku_ready, H_(1, 1))
                act.activation(kq[:, :, :], Gr[:, :, :], ACT.Silu).then_inc(gs_ready, 1)
                act.wait_ge(yt_ready, H_(1, 1))
                dsty = YE[:, 2 * h0:2 * h0 + 2, 0:T] if r is None else YE[:, ds(r * 2 + 2 * h0, 2), 0:T]
                act.activation(dsty, txn[:, 0, :, :], ACT.Copy).then_inc(yh_ready, 1)

            even_head(None, 0, False)
            even_head(None, 1, True)
            with act.Fori(0, 3) as r:
                even_head(r, 2, True)
            even_head(None, 5, False, True)

            def out_projection(n, p0):
                with act.Fori(0, 3) as r:
                    for i in range(2):
                        splits(p0 + 4 * i + 4, 8, r)
                        round_x(n, i, 2, r)
                splits(p0 + 28)
                round_x(n, 6)
                splits(p0 + 32, kinds=("std",) * 3)
                round_x(n, 7)
                split(p0 + 35, 0, None)

            def feed_forward(layer, n, p0, e0):
                for half in range(2):
                    p = p0 + half * (UPP + DNP)
                    e = e0 + half * (2 * GS + 8)
                    s0 = (2 * layer + half) * GS

                    def up(r, j0, kinds, first):
                        q = p + 8 * j0
                        if first:
                            first_step(n, q + 4)
                        else:
                            splits(q + 4, 8, r)
                        copy_low(q + 4, e + 2 * j0, 8, 2, r)
                        splits(q + 8, 8, r, kinds)
                        copy_low(q + 8, e + 2 * j0 + 1, 8, 2, r)
                        act.wait_ge(cws_ready, at(s0 + j0 + 1, 1, r))
                        act.wait_ge(a_ready, at(s0 + j0 + 1, 1, r))
                        for t in range(2):
                            ins = act.activation(cvo[:, 1, t, :], apad[:, 1, t, 2:T + 2], ACT.Identity,
                                                 bias=cws[:, 4 * t + 11:4 * t + 12], scale=cws[:, 4 * t + 10:4 * t + 11])
                        ins.then_inc(vc_ready, 1)
                        act.wait_ge(cv_ready, at(s0 + j0 + 1, 1, r))
                        if s0 + j0:
                            act.wait_ge(hid_ready, at(s0 + j0, 1, r))
                        act.activation(sg[:, :, :], cvo[:, 0, :, :], ACT.Silu).then_inc(silu_ready, 1)
                        act.wait_ge(hid_ready, at(s0 + j0 + 1, 1, r))
                        if r is None:
                            dh = YF[:, 2 * j0:2 * j0 + 2, 0:T]
                        else:
                            dh = YF[:, ds(r * 2 + 2 * j0, 2), 0:T]
                        act.activation(dh, hid[:, :, :], ACT.Copy).then_inc(hh_ready, 1)

                    up(None, 0, ("std",) * 4, half == 0)
                    with act.Fori(0, GS - 2) as r:
                        up(r, 1, ("std",) * 4, False)
                    up(None, GS - 1, ("down",) * 4, False)
                    q = p + UPP
                    with act.Fori(0, 3) as r:
                        for i in range(2):
                            splits(q + 8 * i + 4, 16, r, ("down",) * 8)
                            if half == 1 and n < 3:
                                round_x(n + 1, i, 2, r)
                    splits(q + 52, kinds=("down",) * 8)
                    if half == 1 and n < 3:
                        round_x(n + 1, 6)
                    splits(q + 60, kinds=("down",) * 4)
                    if half == 0:
                        splits(q + 64)
                    elif n < 3:
                        splits(q + 64, kinds=("std",) * 3)
                        round_x(n + 1, 7)
                        split(q + 67, 0, None)

            out_projection(1, OE_P0)
            act.wait_ge(piece_done, F0_P0)
            act.wait_ge(bank_free, F0_E0)
            act.dma_start(cw[:, :, :], A["conv"][0, :, :, :]).then_inc(conv_in, 16)
            feed_forward(0, 1, F0_P0, F0_E0)
            act.wait_ge(piece_done, MD_P0)
            act.wait_ge(bank_free, MD_E0)
            act.dma_start(caus[:, :], A["caus"]).then_inc(odd_loads, 16)
            act.dma_start(mcos[:, :], A["mcos"]).then_inc(odd_loads, 16)
            act.dma_start(msin[:, :], A["msin"]).then_inc(odd_loads, 16)
            act.dma_start(swp[:, :], A["swp"]).then_inc(odd_loads, 16)

            def csquare(j):
                act.wait_ge(c_ready, j + 1)
                if j >= 2:
                    act.wait_ge(csum_done, j - 1)
                act.activation(txn[:, j % 2, :, :], C8[:, 2 * j:2 * j + 2, :], ACT.Square).then_inc(csq_ready, 1)

            def compressed(w):
                act.wait_ge(cvar_ready, w + 1)
                act.activation(nwt[:, 1, :], nwt[:, 0, :], ACT.Sqrt).then_inc(csd_ready, 1)
                for j in range(2):
                    act.wait_ge(ct_ready, 2 * w + j + 1)
                    act.activation(CS[:, 4 * w + 2 * j:4 * w + 2 * j + 2, 0:T], cn[:, j, :, :], ACT.Copy).then_inc(ch_ready, 1)

            q = MD_P0
            splits(q + 4, kinds=("std",) * 2)
            root(2)
            copy_low(q + 2, MD_E0)
            splits(q + 6)
            copy_low(q + 6, MD_E0 + 1)
            csquare(0)
            splits(q + 10)
            copy_low(q + 10, MD_E0 + 2)
            csquare(1)
            splits(q + 14)
            compressed(0)
            copy_low(q + 14, MD_E0 + 3)
            csquare(2)
            splits(q + 18, kinds=("uq", "uq", "std", "std"))
            copy_low(q + 18, MD_E0 + 4)
            csquare(3)
            compressed(1)

            def exponentials(r, c0):
                for h in range(2):
                    act.wait_ge(mx_ready, at(2 * c0 + h + 1, 4, r))
                    act.activation(Sc[:, h, 0:P], Sc[:, h, 0:P], ACT.Exp, bias=st8[:, h, 0:1],
                                   accum_out=st8[:, h, 2:3])
                    act.activation(Sc[:, h, P:3 * P], Sc[:, h, P:3 * P], ACT.Exp, bias=st8[:, h, 1:2],
                                   accum_out=st8[:, h, 3:4]).then_inc(ex_ready, 1)

            def attended(r, c0):
                for h in range(2):
                    act.wait_ge(pt_done, at(2 * c0 + h + 1, 4, r))
                    act.activation(PT[:, h, :], PS[:, 6 + h, 0:3 * P], ACT.Copy).then_inc(pt_ready, 1)
                act.wait_ge(at_done, at(c0 + 1, 2, r))
                dy = YO[:, 2 * c0:2 * c0 + 2, 0:T] if r is None else YO[:, ds(r * 4 + 2 * c0, 2), 0:T]
                act.activation(dy, PS[:, 3, :].rearrange("p (a t) -> p a t", a=2), ACT.Copy).then_inc(ah_ready, 1)

            def pair_body(r, c0, attend, last=False):
                p0 = MP_P0 + 4 * c0
                if c0:
                    splits(p0 + 2, 8, r, ("std",) * 2)
                act.wait_ge(piece_done, at(p0 + 2, 8, r))
                if c0:
                    act.wait_ge(qa_free, at(c0, 2, r))
                act.activation(lo4[:, 0:3, :], PS[:, 0:3, T:2 * T], ACT.Copy).then_inc(qa_copied, 1)
                if attend:
                    exponentials(r, c0 - 1)
                splits(p0 + 4, 8, r, ("std", "std") if last else ("uq", "uq"))
                act.wait_ge(piece_done, at(p0 + 4, 8, r))
                if c0:
                    act.wait_ge(kb_free, at(c0, 2, r))
                act.activation(lo4[:, 3:5, :], PS[:, 3:5, T:2 * T], ACT.Copy).then_inc(kb_copied, 1)
                if attend:
                    attended(r, c0 - 1)
                act.activation(V2[:, :, :], PS[:, 5, :].rearrange("p (a t) -> p a t", a=2),
                               ACT.Copy).then_inc(v2_ready, 1)

            pair_body(None, 0, False)
            with act.Fori(0, 3) as r:
                pair_body(r, 1, True)
                pair_body(r, 2, True)
            pair_body(None, 7, True, True)
            splits(OO_P0 + 2, kinds=("std",) * 2)
            exponentials(None, 7)
            attended(None, 7)

            out_projection(3, OO_P0)
            act.wait_ge(piece_done, F1_P0)
            act.wait_ge(bank_free, F1_E0)
            act.dma_start(cw[:, :, :], A["conv"][1, :, :, :]).then_inc(conv_in, 16)
            feed_forward(1, 3, F1_P0, F1_E0)
            root(4)
            for j in range(8):
                act.wait_ge(fin_ready, j + 1)
                act.dma_start(out[:, 2 * j:2 * j + 2, :], H[:, 2 * j:2 * j + 2, :]).then_inc(stored, 16)
            act.wait_ge(stored, 16 * 8)

        @block.vector
        def _(dve):
            V = nc.vector

            def split(p, s, r, kind="std"):
                u = p // 2
                off, n = geometry(kind, p)
                dve.wait_ge(hi_ready, at(p + 1, s, r))
                V.tensor_tensor(lo[:, p % SLOTS, 0:n], raw[:, u % SLOTS, off:off + n], f(hi[:, p % SLOTS, 0:n]),
                                ALU.subtract).then_inc(lo_ready, 1)

            def splits(p, s=0, r=None, kinds=("std",) * 4):
                for i, k in enumerate(kinds):
                    split(p + i, s, r, k)

            def add_banks(dstap, e, se=0, r=None, l=None):
                dve.wait_ge(lo_copied, at((e if l is None else l) + 1, se, r))
                b = pair(e)
                return V.tensor_tensor(dstap, PS[:, b:b + 2, 0:T], lot[:, :, :], ALU.add)

            def add_residual(p_end, e, sp_, se, r, j0, n=None):
                dve.wait_ge(piece_done, at(p_end, sp_, r))
                b = pair(e)
                h = H[:, 2 * j0:2 * j0 + 2, :] if r is None else H[:, ds(r * 4 + 2 * j0, 2), :]
                V.tensor_tensor(h, h, PS[:, b:b + 2, 0:T], ALU.add)
                dve.drain()
                V.tensor_tensor(h, h, PS[:, b:b + 2, T:2 * T], ALU.add).then_inc(bank_free, 1)
                if n is not None:
                    dve.drain()
                    x_pair(n, j0, r)
                    x_low(n, j0, r)

            def x_pair(n, j, r=None):
                c = (VEC["g_even"], VEC["g_ffn"], VEC["g_odd"], VEC["g_ffn"] + KD)[n] + 2 * j
                for t in range(2):
                    if r is None:
                        h, g = H[:, 2 * j + t, :], vec[:, c + t:c + t + 1]
                    else:
                        h, g = H[:, ds(r * 4 + (2 * j + t), 1), :].rearrange("p a t -> p (a t)"), vec[:, ds(r * 4 + (c + t), 1)]
                    ins = V.tensor_scalar(txn[:, j % 2, t, :], h, g, None, ALU.mult)
                ins.then_inc(xt_ready, 1)

            def x_low(n, j, r=None):
                dve.wait_ge(xh_ready, at(8 * n + j + 1, 2, r))
                x = XS[:, 2 * j:2 * j + 2, :] if r is None else XS[:, ds(r * 4 + 2 * j, 2), :]
                V.tensor_tensor(x[:, :, T:2 * T], txn[:, j % 2, :, :], f(x[:, :, 0:T]), ALU.subtract).then_inc(xl_ready, 1)

            rn2 = rn[:, :].unsqueeze(1).broadcast_to([P, 2, T])

            def add_scaled(d, e, se=0, r=None, l=None):
                add_banks(d, e, se, r, l).then_inc(bank_free, 1)
                dve.drain()
                return V.tensor_tensor(d, d, rn2, ALU.mult)

            def inv_rms(psum, width, var_sem, sd_sem, count, out_=rn[:, :], tmp=nwt[:, 2, :]):
                V.tensor_scalar(nwt[:, 0, :], psum, 1.0 / width, EPS, ALU.mult, ALU.add).then_inc(var_sem, 1)
                dve.wait_ge(sd_sem, count)
                V.reciprocal(out_, nwt[:, 1, :])
                dve.drain()
                V.tensor_tensor(tmp, out_, out_, ALU.mult)
                dve.drain()
                V.scalar_tensor_tensor(out=tmp, in0=tmp, scalar=-0.5, in1=nwt[:, 0, :], op0=ALU.mult, op1=ALU.mult)
                dve.drain()
                V.scalar_tensor_tensor(out=out_, in0=tmp, scalar=1.5, in1=out_, op0=ALU.add, op1=ALU.mult)
                dve.drain()

            def root(n):
                dve.wait_ge(sum_done, n + 1)
                inv_rms(PS[:, 7, 0:T], D, var_ready, sd_ready, n + 1)

            def first_step(n, p):
                splits(p, kinds=("std",) * 2)
                root(n)
                splits(p + 2, kinds=("std",) * 2)

            V.memset(ones[:, :], 1.0).then_inc(ones_set, 1)
            dve.wait_ge(small_in, 32)
            lre, lim = (vec[:, VEC[k]:VEC[k] + KD] for k in ("lre", "lim"))
            V.tensor_tensor(pt[:, 12, :], lre, lre, ALU.mult)
            V.tensor_tensor(pt[:, 13, :], lim, lim, ALU.mult)
            dve.drain()
            V.tensor_tensor(pt[:, 13, :], pt[:, 12, :], pt[:, 13, :], ALU.add)
            dve.drain()
            V.reciprocal(pt[:, 12, :], pt[:, 13, :]).then_inc(den_ready, 1)
            for c in range(4):
                dve.wait_ge(x_in[c], 16)
                dve.drain()
                x_pair(0, 2 * c)
                x_pair(0, 2 * c + 1)
                x_low(0, 2 * c)
                split(c, 0, None)
                x_low(0, 2 * c + 1)
            first_step(0, 4)
            add_scaled(U[:, 0:2, :], 0)
            splits(8)
            add_scaled(U[:, 2:4, :], 1).then_inc(u_ready, 1)
            dve.wait_ge(even_loads, 48)

            def even_head(r, h0, s5, glu=False):
                p0, e0 = 8 + 16 * h0, 2 + 4 * h0
                H_ = lambda c, s: at(c + s * h0, s, r)
                S_ = lambda c, s: at(c + s * (h0 - 1), s, r)

                def rotate(d, e):
                    add_scaled(kq[:, :, :], e, 4, r)
                    dve.drain()
                    ra, rb = txn[:, 0], txn[:, 1]
                    V.tensor_tensor(ra, kq[:, :, :], cosR[:, :].unsqueeze(1).broadcast_to([P, 2, T]), ALU.mult)
                    V.tensor_tensor(rb, kq[:, :, :], sinR[:, :].unsqueeze(1).broadcast_to([P, 2, T]), ALU.mult)
                    dve.drain()
                    V.tensor_tensor(d[:, 0, :], ra[:, 0], rb[:, 1], ALU.subtract)
                    V.tensor_tensor(d[:, 1, :], ra[:, 1], rb[:, 0], ALU.add).then_inc(kq_ready, 1)

                def scan(k):
                    dve.wait_ge(w_ready, S_(k + 1, 2))
                    for ri in range(2):
                        for m in range(2):
                            V.tensor_tensor_scan(sT1[:, ri, m, :], magst[:, m:m + 1].broadcast_to([P, T]),
                                                 sB[:, ri, m, :], 0.0, ALU.mult, ALU.add)
                    dve.drain()
                    eb = E[:, k]
                    V.tensor_tensor(sT2, sT1, eb[:, 0:1].broadcast_to([P, 2, 2, T]), ALU.mult)
                    V.tensor_tensor(sB, sT1, eb[:, 1:2].broadcast_to([P, 2, 2, T]), ALU.mult)
                    dve.drain()
                    V.tensor_tensor(sT1[:, 0], sT2[:, 0], sB[:, 1], ALU.subtract)
                    V.tensor_tensor(sT1[:, 1], sT2[:, 1], sB[:, 0], ALU.add).then_inc(z_ready, 1)

                splits(p0 + 4, 16, r)
                rotate(KRo, e0)
                for i in range(4):
                    split(p0 + 8 + i, 16, r)
                    if s5 and i == 1:
                        scan(0)
                rotate(QRo, e0 + 1)
                splits(p0 + 12, 16, r)
                dve.wait_ge(lo_copied, at(e0 + 3, 4, r))
                V.tensor_scalar(Vr[:, 1, :], PS[:, pair(e0 + 2) + 1, 0:T], rtok[:, 1:2], None, ALU.mult).then_inc(bank_free, 1)
                dve.wait_ge(s_done, H_(1, 1))
                dve.wait_ge(dec_in, H_(16, 16))
                V.tensor_tensor(Pm[:, 0:T], PS[:, 4, 0:T], dec[:, :], ALU.mult)
                V.tensor_tensor(Pm[:, T:T + P], PS[:, 4, T:T + P], dec[:, 0:P], ALU.mult).then_inc(pm_ready, 1)
                if glu:
                    dve.wait_ge(glu_sig, 1)
                    V.tensor_tensor(sigs, sigs, U[:, :, :], ALU.mult).then_inc(glu_mul, 1)
                for i in range(4):
                    split(p0 + 16 + i, 16, r)
                    if s5 and i == 1:
                        scan(1)
                if glu:
                    dve.wait_ge(glu_hi, 1)
                    V.tensor_tensor(Y5[:, :, T:2 * T], sigs, f(Y5[:, :, 0:T]), ALU.subtract).then_inc(glu_lo, 1)
                add_scaled(Gr[:, :, :], e0 + 3, 4, r).then_inc(ku_ready, 1)
                dve.wait_ge(osum_done, H_(1, 1))
                norm_head(H_(1, 1))
                for t in range(2):
                    c = VEC["ret"] + 2 * h0 + t
                    wcol = vec[:, c:c + 1] if r is None else vec[:, ds(r * 2 + c, 1)]
                    V.scalar_tensor_tensor(out=txn[:, 0, t, :], in0=PS[:, 5, t * T:(t + 1) * T], scalar=wcol,
                                           in1=ro, op0=ALU.mult, op1=ALU.mult)
                dve.drain()
                dve.wait_ge(gs_ready, H_(1, 1))
                V.tensor_tensor(txn[:, 0, :, :], txn[:, 0, :, :], kq[:, :, :], ALU.mult).then_inc(yt_ready, 1)
                if s5:
                    dve.wait_ge(c_done, S_(2, 2))
                    k = h0 - 1
                    u = U[:, k, :] if r is None else U[:, ds(r + k, 1), :].rearrange("p a t -> p (a t)")
                    c = VEC["d"] + k
                    V.scalar_tensor_tensor(out=u, in0=u, scalar=vec[:, c:c + 1] if r is None else vec[:, ds(r + c, 1)],
                                           in1=PS[:, 6, 0:T], op0=ALU.mult, op1=ALU.add).then_inc(y5_ready, 1)
                dve.wait_ge(yh_ready, H_(1, 1))
                ye = YE[:, 2 * h0:2 * h0 + 2, :] if r is None else YE[:, ds(r * 2 + 2 * h0, 2), :]
                V.tensor_tensor(ye[:, :, T:2 * T], txn[:, 0, :, :], f(ye[:, :, 0:T]), ALU.subtract).then_inc(yl_ready, 1)

            ro = nwt[:, 2, :]

            def norm_head(count):
                inv_rms(PS[:, 4, 0:T], RD, ovar_ready, osd_ready, count, out_=ro, tmp=sq[:, 0, :])

            dve.wait_ge(rt_ready, 1)
            even_head(None, 0, False)
            even_head(None, 1, True)
            with dve.Fori(0, 3) as r:
                even_head(r, 2, True)
            even_head(None, 5, False, True)

            def out_projection(n, p0, e0):
                with dve.Fori(0, 3) as r:
                    for i in range(2):
                        splits(p0 + 4 * i + 4, 8, r)
                        add_residual(p0 + 4 * i + 4, e0 + i, 8, 2, r, i, n)
                splits(p0 + 28)
                add_residual(p0 + 28, e0 + 6, 0, 0, None, 6, n)
                splits(p0 + 32, kinds=("std",) * 3)
                add_residual(p0 + 32, e0 + 7, 0, 0, None, 7, n)
                split(p0 + 35, 0, None)

            def feed_forward(layer, n, p0, e0, l0):
                for half in range(2):
                    p = p0 + half * (UPP + DNP)
                    e = e0 + half * (2 * GS + 8)
                    l = l0 + half * 2 * GS
                    s0 = (2 * layer + half) * GS

                    def up(r, j0, kinds, first):
                        q = p + 8 * j0
                        if first:
                            first_step(n, q + 4)
                            dve.sem_inc(rn_ready, 1)
                        else:
                            splits(q + 4, 8, r)
                        if s0 + j0:
                            dve.wait_ge(cv_ready, at(s0 + j0, 1, r))
                        add_banks(apad[:, 0, :, 2:T + 2], e + 2 * j0, 2, r, l + 2 * j0).then_inc(bank_free, 1)
                        splits(q + 8, 8, r, kinds)
                        add_scaled(apad[:, 1, :, 2:T + 2], e + 2 * j0 + 1, 2, r, l + 2 * j0 + 1).then_inc(a_ready, 1)
                        dve.wait_ge(vc_ready, at(s0 + j0 + 1, 1, r))
                        for i in (1, 0):
                            for t in range(2):
                                V.scalar_tensor_tensor(out=cvo[:, 1, t, :], in0=apad[:, 1, t, i:T + i],
                                                       scalar=cws[:, 8 + 4 * t + i:9 + 4 * t + i], in1=cvo[:, 1, t, :],
                                                       op0=ALU.mult, op1=ALU.add)
                            dve.drain()
                        dve.wait_ge(silu_ready, at(s0 + j0 + 1, 1, r))
                        V.tensor_tensor(hid[:, :, :], sg[:, :, :], cvo[:, 1, :, :], ALU.mult).then_inc(hid_ready, 1)
                        dve.wait_ge(hh_ready, at(s0 + j0 + 1, 1, r))
                        if r is None:
                            y = YF[:, 2 * j0:2 * j0 + 2, :]
                        else:
                            y = YF[:, ds(r * 2 + 2 * j0, 2), :]
                        V.tensor_tensor(y[:, :, T:2 * T], hid[:, :, :], f(y[:, :, 0:T]), ALU.subtract).then_inc(hl_ready, 1)

                    up(None, 0, ("std",) * 4, half == 0)
                    with dve.Fori(0, GS - 2) as r:
                        up(r, 1, ("std",) * 4, False)
                    up(None, GS - 1, ("down",) * 4, False)
                    q = p + UPP
                    ed = e + 2 * GS
                    m = n + 1 if half == 1 and n < 3 else None
                    with dve.Fori(0, 3) as r:
                        for i in range(2):
                            splits(q + 8 * i + 4, 16, r, ("down",) * 8)
                            add_residual(q + 8 * i + 8, ed + i, 16, 2, r, i, m)
                    splits(q + 52, kinds=("down",) * 8)
                    add_residual(q + 56, ed + 6, 0, 0, None, 6, m)
                    splits(q + 60, kinds=("down",) * 4)
                    if half == 0:
                        splits(q + 64)
                    elif n < 3:
                        splits(q + 64, kinds=("std",) * 3)
                    add_residual(q + 64, ed + 7, 0, 0, None, 7, m)
                    if m is not None:
                        split(q + 67, 0, None)

            out_projection(1, OE_P0, OE_E0)
            V.memset(apad[:, :, :, 0:2], 0.0)
            feed_forward(0, 1, F0_P0, F0_E0, F0_L0)

            def compressed(w):
                dve.wait_ge(csum_done, 2 * w + 2)
                inv_rms(PS[:, 6 + w, 0:T], RANK, cvar_ready, csd_ready, w + 1, out_=rc[:, :])
                g = VEC[("qn", "kvn")[w]]
                for j in range(2):
                    for t in range(2):
                        ins = V.scalar_tensor_tensor(out=cn[:, j, t, :], in0=C8[:, 4 * w + 2 * j + t, :],
                                                     scalar=vec[:, g + 2 * j + t:g + 2 * j + t + 1], in1=rc[:, :],
                                                     op0=ALU.mult, op1=ALU.mult)
                    ins.then_inc(ct_ready, 1)
                for j in range(2):
                    k = 4 * w + 2 * j
                    dve.wait_ge(ch_ready, 2 * w + j + 1)
                    V.tensor_tensor(CS[:, k:k + 2, T:2 * T], cn[:, j, :, :], f(CS[:, k:k + 2, 0:T]),
                                    ALU.subtract).then_inc(cl_ready, 1)
                dve.drain()

            q = MD_P0
            splits(q + 4, kinds=("std",) * 2)
            root(2)
            dve.wait_ge(lo_copied, MD_L0 + 1)
            V.tensor_tensor(KX[:, :], PS[:, pair(MD_E0), 0:T], lot[:, 0, :], ALU.add).then_inc(bank_free, 1)
            dve.drain()
            V.tensor_tensor(KX[:, :], KX[:, :], rn[:, :], ALU.mult).then_inc(kx_ready, 1)
            for j in range(4):
                splits(q + 6 + 4 * j, kinds=("std",) * 4 if j < 3 else ("uq", "uq", "std", "std"))
                if j == 2:
                    compressed(0)
                add_scaled(C8[:, 2 * j:2 * j + 2, :], MD_E0 + 1 + j, l=MD_L0 + 1 + j).then_inc(c_ready, 1)
            compressed(1)
            dve.wait_ge(odd_loads, 64)

            def rotary(dst_, x, swapped):
                dve.drain()
                V.tensor_tensor(rt[:, 0, :], x, mcos[:, :], ALU.mult)
                dve.wait_ge(sw_done, swapped)
                V.tensor_tensor(rt[:, 1, :], PS[:, 2, 0:T], msin[:, :], ALU.mult)
                dve.drain()
                V.tensor_tensor(dst_, rt[:, 0, :], rt[:, 1, :], ALU.add).then_inc(qr_ready, 1)

            def masked_scores(r, c0):
                for h in range(2):
                    dve.wait_ge(sc_done, at(2 * c0 + h + 1, 4, r))
                    if c0:
                        dve.wait_ge(pt_done, at(2 * c0 + h - 1, 4, r))
                    V.scalar_tensor_tensor(out=Sc[:, h, :], in0=PS[:, 6 + h, 0:3 * P], scalar=(MN + MR) ** -0.5,
                                           in1=caus[:, :], op0=ALU.mult, op1=ALU.add)
                    dve.drain()
                    V.tensor_reduce(st8[:, h, 0:1], Sc[:, h, 0:P], AX.X, ALU.max, negate=True)
                    V.tensor_reduce(st8[:, h, 1:2], Sc[:, h, P:3 * P], AX.X, ALU.max, negate=True).then_inc(mx_ready, 1)

            def probabilities(r, c0):
                for h in range(2):
                    dve.wait_ge(ex_ready, at(2 * c0 + h + 1, 4, r))
                    V.reciprocal(st8[:, h, 4:6], st8[:, h, 2:4])
                    dve.drain()
                    V.tensor_scalar(Sc[:, h, 0:P], Sc[:, h, 0:P], st8[:, h, 4:5], None, ALU.mult)
                    V.tensor_scalar(Sc[:, h, P:3 * P], Sc[:, h, P:3 * P], st8[:, h, 5:6], None, ALU.mult)\
                        .then_inc(pn_ready, 1)

            def attended_low(r, c0):
                dve.wait_ge(ah_ready, at(c0 + 1, 2, r))
                y = YO[:, 2 * c0:2 * c0 + 2, :] if r is None else YO[:, ds(r * 4 + 2 * c0, 2), :]
                V.tensor_tensor(y[:, :, T:2 * T], PS[:, 3, :].rearrange("p (a t) -> p a t", a=2), f(y[:, :, 0:T]),
                                ALU.subtract).then_inc(al_ready, 1)

            def pair_body(r, c0, attend, last=False):
                p0 = MP_P0 + 4 * c0
                if c0:
                    splits(p0 + 2, 8, r, ("std",) * 2)
                if attend:
                    masked_scores(r, c0 - 1)
                dve.wait_ge(qa_copied, at(c0 + 1, 2, r))
                V.tensor_tensor(QN[:, :, :], PS[:, 0:2, 0:T], lo4[:, 0:2, :], ALU.add)
                V.tensor_tensor(QX[:, :], PS[:, 2, 0:T], lo4[:, 2, :], ALU.add).then_inc(qa_free, 1)
                if attend:
                    probabilities(r, c0 - 1)
                splits(p0 + 4, 8, r, ("std", "std") if last else ("uq", "uq"))
                dve.wait_ge(kb_copied, at(c0 + 1, 2, r))
                V.tensor_tensor(KN[:, :, :], PS[:, 3:5, 0:T], lo4[:, 3:5, :], ALU.add).then_inc(kb_free, 1)
                if c0 == 0:
                    rotary(KRp[:, :], KX[:, :], 1)
                rotary(QRp[:, :], QX[:, :], at(c0 + 2, 2, r))
                if attend:
                    attended_low(r, c0 - 1)

            pair_body(None, 0, False)
            with dve.Fori(0, 3) as r:
                pair_body(r, 1, True)
                pair_body(r, 2, True)
            pair_body(None, 7, True, True)
            splits(OO_P0 + 2, kinds=("std",) * 2)
            masked_scores(None, 7)
            probabilities(None, 7)
            attended_low(None, 7)

            out_projection(3, OO_P0, OO_E0)
            V.memset(apad[:, :, :, 0:2], 0.0)
            feed_forward(1, 3, F1_P0, F1_E0, F1_L0)

            dve.wait_ge(sum_done, 5)
            inv_rms(PS[:, 7, 0:T], D, var_ready, sd_ready, 5)
            for k in range(KD):
                c = VEC["g_fin"] + k
                ins = V.scalar_tensor_tensor(out=H[:, k, :], in0=H[:, k, :], scalar=vec[:, c:c + 1], in1=rn[:, :],
                                             op0=ALU.mult, op1=ALU.mult)
                if k % 2:
                    ins.then_inc(fin_ready, 1)

        @block.gpsimd
        def _(pool):
            G = nc.gpsimd

            def sum_squares(n, e):
                pool.wait_ge(sum_done, n)
                G.memset(acc[:, :, :], 0.0)
                with pool.Fori(0, 8) as r:
                    pool.drain()
                    pool.wait_ge(bank_free, r + (e + 1))
                    h = H[:, ds(r * 2, 2), :]
                    G.tensor_tensor(sq[:, :, :], h, h, ALU.mult)
                    pool.drain()
                    G.tensor_tensor(acc[:, :, :], acc[:, :, :], sq[:, :, :], ALU.add)
                pool.drain()
                G.memset(mark[:, :], 0.0).then_inc(ssq_ready, 1)

            G.memset(acc[:, :, :], 0.0)
            for c in range(4):
                for i in range(2):
                    pool.drain()
                    if i == 0:
                        pool.wait_ge(sq_ready, c + 1)
                    ins = G.tensor_tensor(acc[:, :, :], acc[:, :, :], (sT1, sT2)[c % 2][:, i], ALU.add)
                ins.then_inc(sq_added, 1)

            def s5_setup():
                lre, lim, ldt = (vec[:, VEC[k]:VEC[k] + KD] for k in ("lre", "lim", "ldt"))
                col = lambda i: pt[:, i, :]

                def tt(o, a, b, op):
                    G.tensor_tensor(o, a, b, op)
                    pool.drain()

                def ts(o, a, s1, s2, o1, o2=None):
                    if o2 is None:
                        G.tensor_scalar(o, a, s1, None, o1)
                    else:
                        G.tensor_scalar(o, a, s1, s2, o1, o2)
                    pool.drain()

                def stt(o, a, s, b, o1, o2):
                    ts(col(14), a, s, None, o1)
                    tt(o, col(14), b, o2)

                MAGIC = 12582912.0

                def exp(o, z, a, b, c):
                    ts(o, z, -150.0, 130.0, ALU.max, ALU.min)
                    ts(a, o, 1.4426950408889634, MAGIC, ALU.mult, ALU.add)
                    ts(a, a, -MAGIC, None, ALU.add)
                    stt(b, a, -0.693359375, o, ALU.mult, ALU.add)
                    stt(b, a, 2.12194440e-4, b, ALU.mult, ALU.add)
                    ts(o, b, 1.0 / 5040, None, ALU.mult)
                    for k in (720, 120, 24, 6, 2, 1):
                        stt(o, o, 1.0 / k, b, ALU.add, ALU.mult)
                    ts(o, o, 1.0, None, ALU.add)
                    ts(b, a, -126.0, 127.0, ALU.max, ALU.min)
                    tt(a, a, b, ALU.subtract)
                    for e_ in (b, a):
                        ts(c, e_, 127.0, 8388608.0, ALU.add, ALU.mult)
                        G.tensor_copy(pti, c)
                        pool.drain()
                        tt(o, o, pti.bitcast(fp32), ALU.mult)

                dt_, mg, th, cs, sn = col(0), col(1), col(2), col(3), col(4)
                a, b, c, d_, e_, g_, h_ = (col(i) for i in range(5, 12))
                exp(dt_, ldt, a, b, c)
                tt(d_, lre, dt_, ALU.mult)
                exp(mg, d_, a, b, c)
                tt(th, lim, dt_, ALU.mult)
                ts(a, th, 2.0 / math.pi, MAGIC, ALU.mult, ALU.add)
                ts(a, a, -MAGIC, None, ALU.add)
                parts, rest = [], math.pi / 2
                for bits in (8, 9, 10):
                    scale = 2.0 ** (bits - 1 - math.floor(math.log2(rest)))
                    v = math.floor(rest * scale) / scale
                    parts.append(v)
                    rest -= v
                parts.append(rest)
                stt(b, a, -parts[0], th, ALU.mult, ALU.add)
                for v in parts[1:]:
                    stt(b, a, -v, b, ALU.mult, ALU.add)
                tt(c, b, b, ALU.mult)
                ts(sn, c, 1.0 / 362880, None, ALU.mult)
                for k in (-5040, 120, -6):
                    stt(sn, sn, 1.0 / k, c, ALU.add, ALU.mult)
                stt(sn, sn, 1.0, b, ALU.add, ALU.mult)
                ts(cs, c, -1.0 / 3628800, None, ALU.mult)
                for k in (40320, -720, 24, -2):
                    stt(cs, cs, 1.0 / k, c, ALU.add, ALU.mult)
                ts(cs, cs, 1.0, None, ALU.add)
                ts(b, a, 0.25, MAGIC, ALU.mult, ALU.add)
                ts(b, b, -MAGIC, None, ALU.add)
                stt(a, b, -4.0, a, ALU.mult, ALU.add)
                ts(b, a, 0.0, None, ALU.is_equal)
                tt(c, a, a, ALU.mult)
                ts(c, c, 4.0, None, ALU.is_equal)
                tt(b, b, c, ALU.subtract)
                ts(c, a, 1.0, None, ALU.is_equal)
                ts(d_, a, -1.0, None, ALU.is_equal)
                tt(c, c, d_, ALU.subtract)
                tt(d_, cs, b, ALU.mult)
                tt(e_, sn, c, ALU.mult)
                tt(d_, d_, e_, ALU.subtract)
                tt(e_, sn, b, ALU.mult)
                tt(g_, cs, c, ALU.mult)
                tt(e_, e_, g_, ALU.add)
                G.tensor_copy(ph[:, 0, 0, :], d_)
                G.tensor_copy(ph[:, 0, 1, :], e_)
                G.tensor_copy(mag[:, :], mg)
                pool.drain()
                for l in range(7):
                    pr, pi_ = ph[:, l, 0, :], ph[:, l, 1, :]
                    tt(a, pr, pr, ALU.mult)
                    tt(b, pi_, pi_, ALU.mult)
                    tt(ph[:, l + 1, 0, :], a, b, ALU.subtract)
                    tt(a, pr, pi_, ALU.mult)
                    ts(ph[:, l + 1, 1, :], a, 2.0, None, ALU.mult)
                tt(a, mg, d_, ALU.mult)
                ts(a, a, -1.0, None, ALU.add)
                tt(b, mg, e_, ALU.mult)
                c = col(12)
                tt(g_, a, lre, ALU.mult)
                tt(h_, b, lim, ALU.mult)
                tt(g_, g_, h_, ALU.add)
                tt(g_, g_, c, ALU.mult)
                tt(h_, b, lre, ALU.mult)
                tt(b, a, lim, ALU.mult)
                tt(h_, h_, b, ALU.subtract)
                tt(h_, h_, c, ALU.mult)
                B = sB.rearrange("p a b t -> p (a b t)").rearrange("p (a m c) -> p a m c", a=2, m=KD)
                o = sT1.rearrange("p a b t -> p (a b t)").rearrange("p (a m c) -> p a m c", a=2, m=KD)
                w = sT2.rearrange("p a b t -> p (a b t)").rearrange("p (a m c) -> p a m c", a=2, m=KD)
                fr = g_.unsqueeze(2).broadcast_to([P, KD, 32])
                fi = h_.unsqueeze(2).broadcast_to([P, KD, 32])
                tt(o[:, 0], B[:, 0], fr, ALU.mult)
                tt(w[:, 0], B[:, 1], fi, ALU.mult)
                tt(o[:, 0], o[:, 0], w[:, 0], ALU.subtract)
                tt(o[:, 1], B[:, 1], fr, ALU.mult)
                tt(w[:, 0], B[:, 0], fi, ALU.mult)
                G.tensor_tensor(o[:, 1], o[:, 1], w[:, 0], ALU.add).then_inc(bb_ready, 1)

            def phasors(k, h0, r):
                m = 4 * h0 + 2 * k
                G.tensor_copy(phst[:, :, :, :], ph[:, :, :, m:m + 2] if r is None else ph[:, :, :, ds(r * 4 + m, 2)])
                e = E[:, k]
                G.memset(e[:, 0, :, 0:1], 1.0)
                G.memset(e[:, 1, :, 0:1], 0.0)
                for l in range(8):
                    n = 1 << l
                    pool.drain()
                    c, s_ = (phst[:, l, ri, :].unsqueeze(1).unsqueeze(3).broadcast_to([P, 2, 2, n]) for ri in range(2))
                    G.tensor_tensor(g1[:, :, :, 0:n], e[:, :, :, 0:n], c, ALU.mult)
                    G.tensor_tensor(g2[:, :, :, 0:n], e[:, :, :, 0:n], s_, ALU.mult)
                    pool.drain()
                    G.tensor_tensor(e[:, 0, :, n:2 * n], g1[:, 0, :, 0:n], g2[:, 1, :, 0:n], ALU.subtract)
                    G.tensor_tensor(e[:, 1, :, n:2 * n], g1[:, 1, :, 0:n], g2[:, 0, :, 0:n], ALU.add)

            def rotate_in(k, h0, r):
                m = 4 * h0 + 2 * k
                pool.drain()
                pool.wait_ge(bu_copied, at(m + 2, 4, r))
                if m:
                    pool.wait_ge(c_done, at(m // 2, 2, r))
                G.tensor_copy(magst[:, :], mag[:, m:m + 2] if r is None else mag[:, ds(r * 4 + m, 2)])
                e = E[:, k]
                G.tensor_tensor(sT1, sB, e[:, 0:1].broadcast_to([P, 2, 2, T]), ALU.mult)
                G.tensor_tensor(sT2, sB, e[:, 1:2].broadcast_to([P, 2, 2, T]), ALU.mult)
                pool.drain()
                G.tensor_tensor(sB[:, 0], sT1[:, 0], sT2[:, 1], ALU.add)
                G.tensor_tensor(sB[:, 1], sT1[:, 1], sT2[:, 0], ALU.subtract).then_inc(w_ready, 1)

            def s5_chunk(h0, r):
                if h0:
                    pool.wait_ge(bu_done, at(4 * h0, 4, r))
                if r is None:
                    G.tensor_copy(Bst[:, :, :], BT[:, h0, :, :])
                    G.tensor_copy(Ust[:, :], U[:, h0, :]).then_inc(staged, 1)
                else:
                    G.tensor_copy(Bst[:, :, :], BT[:, ds(r + h0, 1), :, :].rearrange("p a b c -> p (a b) c"))
                    G.tensor_copy(Ust[:, :], U[:, ds(r + h0, 1), :].rearrange("p a t -> p (a t)")).then_inc(staged, 1)
                phasors(0, h0, r)
                pool.drain()
                pool.wait_ge(cst_in, at(16 * h0 + 16, 16, r))
                G.tensor_tensor(Cst[:, :, 1, :], Cst[:, :, 1, :], minus[:, 0:1].unsqueeze(2).broadcast_to([P, 4, 32]),
                                ALU.mult).then_inc(cneg_ready, 1)
                rotate_in(0, h0, r)
                phasors(1, h0, r)
                rotate_in(1, h0, r)

            G.memset(minus[:, :], -1.0)
            pool.wait_ge(small_in, 32)
            pool.wait_ge(den_ready, 1)
            pool.wait_ge(even_loads, 48)
            s5_setup()
            pool.wait_ge(u_ready, 1)
            pool.wait_ge(bt_ready, 2)
            s5_chunk(0, None)
            with pool.Fori(0, 3) as r:
                s5_chunk(1, r)

            def feed_forward(layer, n, e0):
                for half in range(2):
                    e = e0 + half * (2 * GS + 8)
                    s0 = (2 * layer + half) * GS
                    if half == 0:
                        pool.wait_ge(conv_in, 16 * (layer + 1))
                        pool.wait_ge(rn_ready, layer + 1)

                    def convolve(r, j0):
                        s = GS * half + j0
                        if s0 + j0:
                            pool.wait_ge(hid_ready, at(s0 + j0, 1, r))
                        src = cw[:, s, :] if r is None else cw[:, ds(r + s, 1), :].rearrange("p a c -> p (a c)")
                        G.tensor_copy(cws[:, :], src).then_inc(cws_ready, 1)
                        pool.drain()
                        pool.wait_ge(bank_free, at(e + 2 * j0 + 1, 2, r))
                        G.tensor_tensor(apad[:, 0, :, 2:T + 2], apad[:, 0, :, 2:T + 2],
                                        rn[:, :].unsqueeze(1).broadcast_to([P, 2, T]), ALU.mult)
                        pool.drain()
                        w = lambda i: cws[:, 0:8].rearrange("p (t c) -> p t c", t=2)[:, :, i:i + 1].broadcast_to([P, 2, T])
                        for i in (1, 0):
                            G.tensor_tensor(ctmp[:, i, :, :], apad[:, 0, :, i:T + i], w(i), ALU.mult)
                        for t in range(2):
                            G.tensor_scalar(cvo[:, 0, t, :], apad[:, 0, t, 2:T + 2], cws[:, 4 * t + 2:4 * t + 3],
                                            cws[:, 4 * t + 3:4 * t + 4], ALU.mult, ALU.add)
                        pool.drain()
                        G.tensor_tensor(cvo[:, 0], cvo[:, 0], ctmp[:, 1], ALU.add)
                        pool.drain()
                        G.tensor_tensor(cvo[:, 0], cvo[:, 0], ctmp[:, 0], ALU.add).then_inc(cv_ready, 1)

                    if s0 == 0:
                        convolve(None, 0)
                        with pool.Fori(0, GS - 1) as r:
                            convolve(r, 1)
                    else:
                        with pool.Fori(0, GS) as r:
                            convolve(r, 0)
                sum_squares(n, e0 + 4 * GS + 8)

            sum_squares(1, OE_E0)
            feed_forward(0, 2, F0_E0)
            sum_squares(3, OO_E0)
            feed_forward(1, 4, F1_E0)

        @block.tensor
        def _(pe):
            mm = nc.tensor.matmul

            def tile(p, k, n, c, width=256):
                o = k * width + c
                return hi[:, p % SLOTS, o:o + P], lo[:, p % SLOTS, o:o + P]

            def project(bank, wh, wl, x, first, last):
                mm(PS[:, bank, :], wh, x, start=first, stop=False)
                return mm(PS[:, bank, 0:T], wl, x[:, 0:T], start=False, stop=last)

            def piece(p, s, r):
                pe.wait_ge(lo_ready, at(p + 1, s, r))

            def std_piece(p, i, bank, mov, s=0, r=None, nk=4, pieces=4):
                piece(p, s, r)
                for ft in range(2):
                    for k in range(nk):
                        kk = i * nk + k
                        wh, wl = tile(p, k, nk, ft * P)
                        ins = project(bank + ft, wh, wl, mov(kk), kk == 0, i == pieces - 1 and k == nk - 1)
                ins.then_inc(piece_done, 1)

            def step(p, e, mov, s=0, se=0, r=None, before=None, after=None):
                if e >= 2:
                    pe.wait_ge(bank_free, at(e - 1, se, r))
                for i in range(4):
                    if before:
                        before(i)
                    std_piece(p + i, i, pair(e), mov, s, r)
                    if after:
                        after(i)

            XSk = lambda k: XS[:, k, :]

            def norm_sum(n):
                if n:
                    pe.wait_ge(ssq_ready, n)
                else:
                    pe.wait_ge(sq_added, 4)
                mm(PS[:, 7, 0:T], ones[:, :], acc[:, 0, :], start=True, stop=False)
                mm(PS[:, 7, 0:T], ones[:, :], acc[:, 1, :], start=False, stop=True).then_inc(sum_done, 1)

            def x_split(n):
                return lambda i: pe.wait_ge(xl_ready, 8 * n + 2 * i + 2)

            pe.wait_ge(ones_set, 1)
            step(0, 0, XSk, before=x_split(0), after=lambda i: norm_sum(0) if i == 3 else None)
            step(4, 1, XSk)
            pe.wait_ge(small_in, 32)
            pe.wait_ge(bank_free, 1)
            for t in range(2):
                ins = mm(PS[:, 7, T + t:T + t + 1], rn[:, t * P:(t + 1) * P], ident[:, 0:1], start=True, stop=True)
            ins.then_inc(rt_done, 1)

            def b_transposed():
                pe.wait_ge(bb_ready, 1)
                pe.wait_ge(rt_ready, 1)
                ob = sT1.rearrange("p a b t -> p (a b t)").rearrange("p (a m) -> p a m", a=2)
                for k in range(KR):
                    for ri in range(2):
                        i = 2 * k + ri
                        ins = pe.transpose(PS[:, 6 + i // 4, (i % 4) * P:(i % 4 + 1) * P], ob[:, ri, k * P:(k + 1) * P],
                                           ident[:, :])
                ins.then_inc(bt_psum, 8)

            def even_head(r, h0, s5, glu=False):
                p0, e0 = 8 + 16 * h0, 2 + 4 * h0
                H_ = lambda c, s: at(c + s * h0, s, r)
                S_ = lambda c, s: at(c + s * (h0 - 1), s, r)

                def b_u(m):
                    if m == 0:
                        pe.wait_ge(staged, S_(1, 1))
                    if h0 - 1 + m > 0:
                        pe.wait_ge(bu_copied, S_(m, 4))
                    for ri in range(2):
                        ins = mm(PS[:, 7, ri * T:(ri + 1) * T], Bst[32 * m:32 * m + 32, ri, :], Ust[32 * m:32 * m + 32, :],
                                 start=True, stop=True)
                    ins.then_inc(bu_done, 1)

                def c_x(k):
                    pe.wait_ge(z_ready, S_(k + 1, 2))
                    if k == 0:
                        pe.wait_ge(cneg_ready, S_(1, 1))
                        if h0 > 1:
                            pe.wait_ge(y5_ready, S_(0, 1))
                    for m in range(2):
                        q = 2 * k + m
                        for ri in range(2):
                            ins = mm(PS[32 * q:32 * q + 32, 6, 0:T], Cst[:, q, ri, :], sT1[:, ri, m, :],
                                     start=ri == 0, stop=ri == 1)
                    ins.then_inc(c_done, 1)

                def after_k(i):
                    if s5 and i < 2:
                        b_u(i)

                def after_q(t):
                    if glu:
                        pe.wait_ge(ge_ready, 1)
                        pe.wait_ge(gluw_in, 16)
                        for k in range(KR):
                            ins = mm(PS[:, 6 + t // 2, (t % 2) * T:(t % 2 + 1) * T], gluw[:, k, t * P:(t + 1) * P], U[:, k, :],
                                     start=k == 0, stop=k == KR - 1)
                        ins.then_inc(glu_done, 1)

                step(p0, e0, XSk, 16, 4, r, after=after_k)
                step(p0 + 4, e0 + 1, XSk, 16, 4, r, after=after_q)
                pe.wait_ge(bank_free, at(e0 + 1, 4, r))
                b = pair(e0 + 2)
                for i in range(4):
                    p = p0 + 8 + i
                    piece(p, 16, r)
                    for tt in range(2):
                        for k in range(4):
                            kk = 4 * i + k
                            xh = XS[:, kk, tt * P:(tt + 1) * P]
                            xl = XS[:, kk, T + tt * P:T + (tt + 1) * P]
                            wh, wl = hi[:, p % SLOTS, k * T:(k + 1) * T], lo[:, p % SLOTS, k * T:(k + 1) * T]
                            mm(PS[:, b + tt, 0:T], xh, wh, start=kk == 0, stop=False)
                            mm(PS[:, b + tt, 0:T], xh, wl, start=False, stop=False)
                            ins = mm(PS[:, b + tt, 0:T], xl, wh, start=False, stop=kk == KD - 1)
                    ins.then_inc(piece_done, 1)
                    if s5:
                        if i == 0:
                            c_x(0)
                        if i in (1, 2):
                            b_u(i + 1)
                pe.wait_ge(kq_ready, H_(2, 2))
                if h0:
                    pe.wait_ge(ovar_ready, H_(0, 1))
                for k in range(2):
                    mm(PS[:, 4, 0:T], KRo[:, k, 0:P], QRo[:, k, :], start=k == 0, stop=k == 1)
                for k in range(2):
                    ins = mm(PS[:, 4, T:T + P], KRo[:, k, P:T], QRo[:, k, P:T], start=k == 0, stop=k == 1)
                ins.then_inc(s_done, 1)

                def after_g(i):
                    if i == 1:
                        pe.wait_ge(pm_ready, H_(1, 1))
                        pe.wait_ge(lo_copied, at(e0 + 3, 4, r))
                        pe.wait_ge(bank_free, at(e0 + 3, 4, r))
                        if h0:
                            pe.wait_ge(yt_ready, H_(0, 1))
                        for t in range(2):
                            mm(PS[:, 5, t * T:(t + 1) * T], Vr[:, 0, t * P:(t + 1) * P], Pm[:, 0:T], start=True, stop=False)
                            ins = mm(PS[:, 5, t * T + P:(t + 1) * T], Vr[:, 1, t * P:(t + 1) * P], Pm[:, T:T + P],
                                     start=False, stop=True)
                        ins.then_inc(o_done, 1)
                    if i == 3:
                        pe.wait_ge(osq_ready, H_(1, 1))
                        for t in range(2):
                            ins = mm(PS[:, 4, 0:T], ones[:, :], sq[:, t, :], start=t == 0, stop=t == 1)
                        ins.then_inc(osum_done, 1)
                        if s5:
                            c_x(1)
                    if i == 0 and h0 == 0:
                        b_transposed()

                step(p0 + 12, e0 + 3, XSk, 16, 4, r, after=after_g)

            even_head(None, 0, False)
            even_head(None, 1, True)
            with pe.Fori(0, 3) as r:
                even_head(r, 2, True)
            even_head(None, 5, False, True)

            YEk = lambda k: Y5[:, k, :] if k < KR else YE[:, k - KR, :]
            YOk = lambda k: YO[:, k, :]

            def out_projection(p0, e0, mov, before):
                step(p0, e0, mov, before=before)
                step(p0 + 4, e0 + 1, mov)
                with pe.Fori(0, 3) as r:
                    for i in range(2, 4):
                        step(p0 + 4 * i, e0 + i, mov, 8, 2, r)

            def feed_forward(layer, n, p0, e0):
                for half in range(2):
                    p = p0 + half * (UPP + DNP)
                    e = e0 + half * (2 * GS + 8)
                    s0 = (2 * layer + half) * GS
                    j0 = 0
                    if half == 0:
                        step(p, e, XSk, before=x_split(n), after=lambda i: norm_sum(n) if i == 2 else None)
                        step(p + 4, e + 1, XSk)
                        j0 = 1
                    with pe.Fori(0, GS - j0) as r:
                        step(p + 8 * j0, e + 2 * j0, XSk, 8, 2, r)
                        step(p + 8 * j0 + 4, e + 2 * j0 + 1, XSk, 8, 2, r)
                    q, ed = p + UPP, e + 2 * GS

                    def down(i0, r):
                        pe.wait_ge(bank_free, at(ed + i0 - 1, 2, r))
                        for i in range(8):
                            pc = q + 8 * i0 + i
                            u, part = i // 2, i % 2
                            piece(pc, 16, r)
                            if r is None and i0 == 0 and u in (0, 2) and part == 0:
                                pe.wait_ge(hl_ready, s0 + (GS // 2 + 1, GS)[u // 2])
                            ft = u % 2
                            for k in range((6, 5)[part]):
                                kk = (u // 2) * GS + part * 6 + k
                                ins = project(pair(ed + i0) + ft, hi[:, pc % SLOTS, k * P:(k + 1) * P],
                                              lo[:, pc % SLOTS, k * P:(k + 1) * P], YF[:, kk, :], kk == 0, kk == GK - 1)
                            ins.then_inc(piece_done, 1)

                    down(0, None)
                    down(1, None)
                    with pe.Fori(0, 3) as r:
                        down(2, r)
                        down(3, r)

            def even_inputs(i):
                if i == 0:
                    pe.wait_ge(glu_lo, 1)
                if i in (1, 3):
                    pe.wait_ge(yl_ready, RH - (i == 1))

            out_projection(OE_P0, OE_E0, YEk, even_inputs)
            feed_forward(0, 1, F0_P0, F0_E0)

            q = MD_P0

            def c_squares(j):
                pe.wait_ge(csq_ready, j + 1)
                for t in range(2):
                    ins = mm(PS[:, 6 + j // 2, 0:T], ones[:, :], txn[:, j % 2, t, :], start=j % 2 == 0 and t == 0,
                             stop=j % 2 == 1 and t == 1)
                ins.then_inc(csum_done, 1)

            for i in range(2):
                pc = q + i
                pe.wait_ge(xl_ready, 8 * 2 + 4 * i + 4)
                piece(pc, 0, None)
                if i == 0:
                    pe.wait_ge(bank_free, MD_E0 - 1)
                for k in range(8):
                    kk = 8 * i + k
                    ins = project(pair(MD_E0), hi[:, pc % SLOTS, k * P:(k + 1) * P], lo[:, pc % SLOTS, k * P:(k + 1) * P],
                                  XS[:, kk, :], kk == 0, kk == KD - 1)
                ins.then_inc(piece_done, 1)

            def swap(x, ready, count):
                pe.wait_ge(ready, count)
                mm(PS[:, 2, 0:T], swp[:, :], x, start=True, stop=True).then_inc(sw_done, 1)

            step(q + 2, MD_E0 + 1, XSk, after=lambda i: norm_sum(2) if i == 0 else None)
            step(q + 6, MD_E0 + 2, XSk, after=lambda i: c_squares(0) if i == 2 else None)
            step(q + 10, MD_E0 + 3, XSk, after=lambda i: c_squares(1) if i == 2 else None)
            step(q + 14, MD_E0 + 4, XSk, after=lambda i: c_squares(2) if i == 2 else None)

            def queries(p0, c0, r):
                pe.wait_ge(lo_ready, at(p0 + 2, 8, r))
                if c0:
                    pe.wait_ge(qr_ready, at(c0 + 1, 2, r))
                else:
                    pe.wait_ge(bank_free, MD_E0 + 5)
                if c0 == 0:
                    pe.wait_ge(cl_ready, 2)
                for b in range(3):
                    for k in range(KR):
                        pc = p0 + k // 2
                        o = (k % 2) * 3 * P + b * P
                        ins = project(b, hi[:, pc % SLOTS, o:o + P], lo[:, pc % SLOTS, o:o + P], CS[:, k, :], k == 0, k == KR - 1)
                ins.then_inc(piece_done, 2)
                if c0 == 0:
                    c_squares(3)

            def keys_values(p0, c0, r):
                pe.wait_ge(lo_ready, at(p0 + 4, 8, r))
                if c0 == 0:
                    pe.wait_ge(cl_ready, 4)
                else:
                    pe.wait_ge(v2_ready, at(c0, 2, r))
                    pe.wait_ge(kb_free, at(c0, 2, r))
                w = lambda x, k: x[:, (p0 + 2 + k // 2) % SLOTS, (k % 2) * 512:(k % 2 + 1) * 512].rearrange("p (h c) -> p h c", h=2)
                for h in range(2):
                    for k in range(KR):
                        project(3 + h, w(hi, k)[:, h, 0:P], w(lo, k)[:, h, 0:P], CS[:, 4 + k, :], k == 0, k == KR - 1)
                for tt in range(2):
                    o = PS[:, 5, tt * T:(tt + 1) * T]
                    for k in range(KR):
                        xh, xl = CS[:, 4 + k, tt * P:(tt + 1) * P], CS[:, 4 + k, T + tt * P:T + (tt + 1) * P]
                        mm(o, xh, w(hi, k)[:, :, P:2 * P], start=k == 0, stop=False)
                        mm(o, xh, w(lo, k)[:, :, P:2 * P], start=False, stop=False)
                        ins = mm(o, xl, w(hi, k)[:, :, P:2 * P], start=False, stop=k == KR - 1)
                ins.then_inc(piece_done, 2)

            def scores(c0, r):
                pe.wait_ge(kb_free, at(c0 + 1, 2, r))
                pe.wait_ge(qr_ready, at(c0 + 2, 2, r))
                for h in range(2):
                    if c0:
                        pe.wait_ge(pt_ready, at(2 * c0 + h - 1, 4, r))
                    R = slice(MR * h, MR * h + MR)
                    for qt in range(2):
                        o = PS[:, 6 + h, 0:P] if qt == 0 else PS[:, 6 + h, P:3 * P]
                        n = P * (qt + 1)
                        mm(o, QN[:, h, qt * P:(qt + 1) * P], KN[:, h, 0:n], start=True, stop=False)
                        ins = mm(o, QRp[R, qt * P:(qt + 1) * P], KRp[R, 0:n], start=False, stop=True)
                    ins.then_inc(sc_done, 1)

            def attend(c0, r, kb):
                for h in range(2):
                    pe.wait_ge(pn_ready, at(2 * c0 + h + 1, 4, r))
                    for i in range(3):
                        ins = pe.transpose(PS[:, 6 + h, i * P:(i + 1) * P], Sc[:, h, i * P:(i + 1) * P], ident[:, :])
                    ins.then_inc(pt_done, 1)
                pe.wait_ge(v2_ready, at(c0 + 1, 2, r))
                pe.wait_ge(kb_free, at(kb, 2, r))
                for h in range(2):
                    pe.wait_ge(pt_ready, at(2 * c0 + h + 1, 4, r))
                    mm(PS[:, 3, h * T:(h + 1) * T], V2[:, 0, h * P:(h + 1) * P], PT[:, h, 0:T], start=True, stop=False)
                    ins = mm(PS[:, 3, h * T + P:(h + 1) * T], V2[:, 1, h * P:(h + 1) * P], PT[:, h, T:3 * P],
                             start=False, stop=True)
                ins.then_inc(at_done, 1)

            def pair_body(r, c0, prev):
                p0 = MP_P0 + 4 * c0
                queries(p0, c0, r)
                if prev:
                    scores(c0 - 1, r)
                keys_values(p0, c0, r)
                if c0 == 0:
                    pe.wait_ge(odd_loads, 64)
                    pe.wait_ge(qa_free, 1)
                    swap(KX[:, :], kx_ready, 1)
                    pe.wait_ge(qr_ready, 1)
                swap(QX[:, :], qa_free, at(c0 + 1, 2, r))
                if prev:
                    attend(c0 - 1, r, c0 + 1)

            pair_body(None, 0, False)
            with pe.Fori(0, 3) as r:
                pair_body(r, 1, True)
                pair_body(r, 2, True)
            pair_body(None, 7, True)
            scores(7, None)
            attend(7, None, 8)

            def odd_inputs(i):
                if i in (0, 3):
                    pe.wait_ge(al_ready, (7, 8)[i == 3])
                if i == 0:
                    pe.wait_ge(v2_ready, 8)
            out_projection(OO_P0, OO_E0, YOk, odd_inputs)
            feed_forward(1, 3, F1_P0, F1_E0)
            norm_sum(4)


def tables():
    t = np.arange(T, dtype=np.float32)

    def rope(dim):
        inv = np.power(np.float32(10000.0), -np.arange(0, dim, 2, dtype=np.float32) / np.float32(dim))
        ang = (t[None, :] * inv[:, None]).astype(np.float32)
        return np.cos(ang).astype(np.float32), np.sin(ang).astype(np.float32)

    cosR, sinR = rope(RD)
    c, s = rope(MR)
    j, i = np.arange(P)[:, None], np.arange(T)[None, :]
    lg = np.log(1.0 - 2.0 ** (-5.0 - np.arange(RH, dtype=np.float64)))
    dec = np.where(i >= j, np.exp(np.maximum(i - j, 0)[None] * lg[:, None, None]), 0.0) * RD ** -0.5
    q = np.arange(P)[:, None]
    tri = np.where(q >= np.arange(P)[None, :], 0.0, -1e30)
    caus = np.concatenate([tri, np.zeros((P, P)), tri], axis=1)
    swp = np.zeros((P, P))
    for m in range(P):
        swp[(m // MR) * MR + (m + MR // 2) % MR, m] = 1.0
    f = lambda a: np.ascontiguousarray(a, dtype=np.float32)
    return {"cosR": f(cosR), "sinR": f(sinR), "mcos": f(np.concatenate([c, c, c, c])),
            "msin": f(np.concatenate([-s, s, -s, s])), "dec": f(dec), "caus": f(caus), "swp": f(swp),
            "ident": f(np.eye(P))}


def kernel(**inputs):
    from concourse import bacc
    from concourse.bass_utils import run_bass_kernel_spmd

    a = {k: np.asarray(v) for k, v in inputs.items()}
    ct = np.ascontiguousarray

    def columns(v):
        return v.reshape(-1, P).T

    def units(w, k, n):
        rows, cols = w.shape
        w = w.reshape(rows // (k * P), k, P, cols // n, n)
        return ct(w.transpose(3, 0, 2, 1, 4).reshape(-1, P, k * n))

    wi = a["w_in_even"][0]
    sec = lambda i, h: wi[:, S5W + i * RH * RD + h * RD:S5W + i * RH * RD + (h + 1) * RD]
    w_in = np.concatenate([wi[:, :S5W]] + [sec(i, h) for h in range(RH) for i in (1, 0, 2, 3)], axis=1)
    dn = a["mla_w_down"][0]
    kr = dn[:, 2 * RANK:]
    uq = a["mla_w_uq"][0].reshape(RANK, MH // 2, 2, MN + MR)
    w_uq = np.concatenate([uq[..., :MN].reshape(RANK, MH // 2, -1), uq[..., MN:].reshape(RANK, MH // 2, -1)],
                          axis=2).reshape(RANK, -1)
    data = {
        "x": ct(a["x"][0].T.reshape(KD, P, T).transpose(1, 0, 2)),
        "w_in": units(w_in, 8, 256),
        "w_oe": units(a["w_out_even"][0], 8, 256),
        "w_oo": units(a["w_out_odd"][0], 8, 256),
        "mla_dn": np.concatenate([units(np.concatenate([kr, kr], axis=1), 16, P),
                                  units(dn[:, :2 * RANK], 8, 256)]),
        "w_uq": units(w_uq, 4, 2 * (MN + MR)),
        "w_ukv": units(a["mla_w_ukv"][0], 4, 2 * (MN + MV)),
    }
    up, down = [], []
    for l in range(2):
        w = a["ffn_w_up"][l].reshape(D, 2, FS, 256)
        up.append(units(ct(w.transpose(0, 2, 1, 3)).reshape(D, 2 * DFF), 8, 256))
        w = a["ffn_w_down"][l].reshape(2, 2, GS, P, 8, 2, P)
        down.append(w.transpose(0, 4, 1, 5, 3, 2, 6).reshape(-1, P, GS * P))
    data["ffn_up"], data["ffn_dn"] = np.concatenate(up), ct(np.concatenate(down))
    cwt = np.concatenate([a["ffn_conv_w"], a["ffn_conv_b"][:, None, :]], axis=1)
    data["conv"] = ct(cwt.reshape(2, 4, 2, FS, 2, P).transpose(0, 5, 3, 2, 4, 1).reshape(2, P, FS, 16))
    ldt = np.repeat(a["s5_log_dt"][0][:, None], S5P, axis=1).reshape(-1)
    data["vec"] = ct(np.concatenate([columns(v.reshape(-1)) for v in (
        a["ln_mix_even"], a["ln_mix_odd"], a["ln_ffn"], a["ln_final"], a["ret_norm"], a["s5_d"], a["s5_glu_b"],
        a["mla_q_norm"], a["mla_kv_norm"], a["s5_lambda_re"], a["s5_lambda_im"], ldt)], axis=1))
    b = np.zeros((P, 2, KD, 2, S5H), np.float32)
    c = np.zeros((KR, P, 4, 2, 2, S5H), np.float32)
    for ri, n in enumerate(("re", "im")):
        bg = a["s5_b_" + n][0].reshape(KD, 2, S5P, S5H)
        cg = a["s5_c_" + n][0].reshape(KR, 4, 2, S5H, S5P)
        for g in range(2):
            b[g * S5P:(g + 1) * S5P, ri, :, g, :] = bg[:, g].transpose(1, 0, 2)
            c[:, g * S5P:(g + 1) * S5P, :, ri, g, :] = cg[:, :, g].transpose(0, 3, 1, 2)
    data["s5b"], data["s5c"] = b.reshape(P, -1), c.reshape(KR, P, -1)
    data["gluw"] = ct(a["s5_glu_w"][0].reshape(KR, P, S5W).transpose(1, 0, 2))
    data.update(tables())

    nc = bacc.Bacc("TRN2", target_bir_lowering=False, num_devices=1)
    A = {k: nc.dram_tensor("in_" + k, v.shape, mybir.dt.from_np(v.dtype), kind="ExternalInput").ap()
         for k, v in data.items()}
    out = nc.dram_tensor("out", (P, KD, T), mybir.dt.float32, kind="ExternalOutput").ap()
    build(nc, A, out)
    r = run_bass_kernel_spmd(nc, [{"in_" + k: v for k, v in data.items()}], core_ids=[0])
    y = r.results[0]["out"]
    return ct(y.transpose(2, 1, 0).reshape(1, T, D))
```

```python
import math
from contextlib import ExitStack

import numpy as np
import concourse.bass as bass
from concourse import mybir

P = 128
T = 256
D = 2048
KD = D // P
S5W, S5G, S5H, S5P = 512, 32, 16, 64
RH, RD = 6, 256
MH, MN, MR, MV = 16, 128, 64, 128
RANK = 512
KR = RANK // P
DFF = 5632
FS = DFF // 256
GS = FS // 2
GK = 2 * GS
EPS = 1e-6
SLOTS = 4

VEC = {}
_c = 0
for _n, _w in (("g_even", KD), ("g_odd", KD), ("g_ffn", 2 * KD), ("g_fin", KD), ("ret", 2 * RH), ("d", KR),
               ("glub", KR), ("qn", KR), ("kvn", KR), ("lre", KD), ("lim", KD), ("ldt", KD)):
    VEC[_n] = _c
    _c += _w
NVEC = _c

IN_P0, IN_E0 = 0, 0
OE_P0, OE_E0 = IN_P0 + 104, IN_E0 + 26
UPP, DNP = 8 * GS, 8 * 8
F0_P0, F0_E0 = OE_P0 + 32, OE_E0 + 8
MD_P0, MD_E0 = F0_P0 + 2 * (UPP + DNP), F0_E0 + 2 * (2 * GS + 8)
MP_P0 = MD_P0 + 18
OO_P0, OO_E0 = MP_P0 + 32, MD_E0 + 5
F1_P0, F1_E0 = OO_P0 + 32, OO_E0 + 8
F0_L0, MD_L0, F1_L0 = 26, 26 + 4 * GS, 31 + 4 * GS
END_P = F1_P0 + 2 * (UPP + DNP)


def at(c, s=0, r=None):
    return c if r is None else r * s + c


def build(nc, A, out):
    fp32, f32r, i32 = mybir.dt.float32, mybir.dt.float32r, mybir.dt.int32
    ALU, ACT, AX = mybir.AluOpType, mybir.ActivationFunctionType, mybir.AxisListType
    ds = bass.ds
    f = lambda ap: ap.bitcast(fp32)

    ctx = ExitStack()
    with ctx:
        def sb(name, shape, dt=fp32, c=ctx):
            return c.enter_context(nc.sbuf_tensor(name, shape, dt))

        def sem(name):
            return ctx.enter_context(nc.semaphore(name))

        H = sb("H", [P, KD, T])
        XS = sb("XS", [P, KD, 2 * T], f32r)
        raw = sb("raw", [P, SLOTS, 2048])
        hi = sb("hi", [P, SLOTS, 1024], f32r)
        lo = sb("lo", [P, SLOTS, 1024], f32r)
        vec = sb("vec", [P, NVEC])
        ident = sb("ident", [P, P])
        ones = sb("ones", [P, P])
        acc = sb("acc", [P, 2, T])
        rn = sb("rn", [P, T])
        lot = sb("lot", [P, 2, T])
        txn = sb("txn", [P, 2, 2, T])
        sq = sb("sq", [P, 2, T])
        rtok = sb("rtok", [P, 2])
        mark = sb("mark", [P, 1])
        nwt = sb("nwt", [P, 3, T])

        even = ExitStack()
        YE = sb("YE", [P, 12, 2 * T], f32r, even)
        s5o = ExitStack()
        E = sb("E", [P, 2, 2, 2, T], fp32, s5o)
        s5o.close()
        Y5 = sb("Y5", [P, KR, 2 * T], f32r, even)
        cosR = sb("cosR", [P, T], fp32, even)
        sinR = sb("sinR", [P, T], fp32, even)
        dec = sb("dec", [P, T], fp32, even)
        KRo = sb("KRo", [P, 2, T], fp32, even)
        QRo = sb("QRo", [P, 2, T], fp32, even)
        Vr = sb("Vr", [P, 2, T], fp32, even)
        Gr = sb("Gr", [P, 2, T], fp32, even)
        Pm = sb("Pm", [P, T + P], fp32, even)
        kq = sb("kq", [P, 2, T], fp32, even)
        S = sb("S", [P, 3, 2, 2, T], fp32, even)
        sB, sT1, sT2 = S[:, 0], S[:, 1], S[:, 2]
        gluw = S[:, :, :, :, :].rearrange("p a b c t -> p (a b c t)")[:, 0:KR * S5W]\
            .rearrange("p (k n) -> p k n", k=KR)
        g1 = sb("g1", [P, 2, 2, T // 2], fp32, even)
        g2 = sb("g2", [P, 2, 2, T // 2], fp32, even)
        U = sb("U", [P, KR, T], fp32, even)
        BT = sb("BT", [P, KR, 2, P], fp32, even)
        Bst = sb("Bst", [P, 2, P], fp32, even)
        Cst = sb("Cst", [P, 4, 2, 32], fp32, even)
        Ust = sb("Ust", [P, T], fp32, even)
        ph = sb("ph", [P, 8, 2, KD], fp32, even)
        mag = sb("mag", [P, KD], fp32, even)
        minus = sb("minus", [P, 1], fp32, even)
        phst = sb("phst", [P, 8, 2, 2], fp32, even)
        magst = sb("magst", [P, 2], fp32, even)
        even.close()
        Ef = E[:, 1].rearrange("p a b t -> p (a b t)")
        pt = Ef[:, 0:32 * KD].rearrange("p (n c) -> p n c", c=KD)
        pti = Ef[:, 32 * KD:33 * KD].bitcast(i32)
        sigs = sT2.rearrange("p a b t -> p (a b) t")

        odd = ExitStack()
        YO = sb("YO", [P, KD, 2 * T], f32r, odd)
        CS = sb("CS", [P, 2 * KR, 2 * T], f32r, odd)
        C8 = sb("C8", [P, 8, T], fp32, odd)
        caus = sb("caus", [P, 3 * P], fp32, odd)
        mcos = sb("mcos", [P, T], fp32, odd)
        msin = sb("msin", [P, T], fp32, odd)
        swp = sb("swp", [P, P], fp32, odd)
        QN = sb("QN", [P, 2, T], fp32, odd)
        KN = sb("KN", [P, 2, T], fp32, odd)
        QX = sb("QX", [P, T], fp32, odd)
        QRp = sb("QRp", [P, T], fp32, odd)
        KX = sb("KX", [P, T], fp32, odd)
        KRp = sb("KRp", [P, T], fp32, odd)
        rt = sb("rt", [P, 2, T], fp32, odd)
        lo4 = sb("lo4", [P, 5, T], fp32, odd)
        st8 = sb("st8", [P, 2, 6], fp32, odd)
        rc = sb("rc", [P, T], fp32, odd)
        cn = sb("cn", [P, 2, 2, T], fp32, odd)
        odd.close()
        Cf = C8[:, :, :].rearrange("p k t -> p (k t)")
        V2 = Cf[:, 0:4 * P].rearrange("p (h n) -> p h n", h=2)
        Sc = Cf[:, 4 * P:10 * P].rearrange("p (h n) -> p h n", h=2)
        PT = Cf[:, 10 * P:16 * P].rearrange("p (h n) -> p h n", h=2)

        ffn = ExitStack()
        YF = sb("YF", [P, GK, 2 * T], f32r, ffn)
        apad = sb("apad", [P, 2, 2, T + 2], fp32, ffn)
        cvo = sb("cvo", [P, 2, 2, T], fp32, ffn)
        sg = sb("sg", [P, 2, T], fp32, ffn)
        hid = sb("hid", [P, 2, T], fp32, ffn)
        cw = sb("cw", [P, FS, 16], fp32, ffn)
        cws = sb("cws", [P, 16], fp32, ffn)
        ctmp = sb("ctmp", [P, 2, 2, T], fp32, ffn)
        XF = sb("XF", [P, KD, T], fp32, ffn)
        ffn.close()

        rnb = rn[:, :].unsqueeze(1).broadcast_to([P, 2, T])
        FINAL_DVE = 5

        PS = ctx.enter_context(nc.psum_tensor("PS", [P, 8, 512], fp32))

        raw_full = [sem(f"raw_full{i}") for i in range(SLOTS)]
        hi_ready = sem("hi_ready")
        lo_ready = sem("lo_ready")
        piece_done = sem("piece_done")
        lo_copied = sem("lo_copied")
        bank_free = sem("bank_free")
        x_in = [sem(f"x_in{i}") for i in range(4)]
        small_in = sem("small_in")
        ones_set = sem("ones_set")
        sq_ready = sem("sq_ready")
        sq_added = sem("sq_added")
        ssq_ready = sem("ssq_ready")
        sum_done = sem("sum_done")
        last_sq = sem("last_sq")
        fin_pool = sem("fin_pool")
        var_ready = sem("var_ready")
        sd_ready = sem("sd_ready")
        rn_ready = sem("rn_ready")
        rt_done = sem("rt_done")
        rt_ready = sem("rt_ready")
        a_ready = sem("a_ready")
        xt_ready = sem("xt_ready")
        xh_ready = sem("xh_ready")
        xl_ready = sem("xl_ready")

        block = ctx.enter_context(nc.Block())
        pair = lambda e: 2 * ((e + (e >= OO_E0)) % 2)

        @block.sync
        def _(sp):
            def load(u, s, r, src, n):
                if u >= SLOTS:
                    sp.wait_ge(lo_ready, at(2 * (u - SLOTS) + 2, 2 * s, r))
                sp.dma_start(raw[:, u % SLOTS, 0:n], src).then_inc(raw_full[u % SLOTS], 16)

            def stream(name, p0, units, n, base=0):
                u0, w = p0 // 2, A[name]
                turns = units // 4
                with sp.Fori(0, turns) as r:
                    for i in range(4):
                        load(u0 + i, 4, r, w[ds(r * 4 + (base + i), 1), :, :].rearrange("a p n -> p (a n)"), n)
                for i in range(4 * turns, units):
                    load(u0 + i, 0, None, w[base + i, :, :], n)

            def feed_forward(layer, p0):
                for half in range(2):
                    p = p0 + half * (UPP + DNP)
                    stream("ffn_up", p, 4 * GS, 2048, (2 * layer + half) * 4 * GS)
                    stream("ffn_dn", p + UPP, 32, 11 * P, (2 * layer + half) * 32)

            for kind, i in ("x0", "w0", "x1", "x2", "w1", "x3", "w2", "w3"):
                i = int(i)
                if kind == "x":
                    sp.dma_start(H[:, 4 * i:4 * i + 4, :], A["x"][:, 4 * i:4 * i + 4, :]).then_inc(x_in[i], 16)
                else:
                    load(i, 0, None, A["w_in"][i, :, :], 2048)
            with sp.Fori(0, 12) as r:
                for i in range(4):
                    load(4 + i, 4, r, A["w_in"][ds(r * 4 + (4 + i), 1), :, :].rearrange("a p n -> p (a n)"), 2048)
            stream("w_oe", OE_P0, 16, 2048)
            feed_forward(0, F0_P0)
            stream("mla_dn", MD_P0, 9, 2048)
            u0 = MP_P0 // 2
            load(u0, 0, None, A["w_ukv"][0, :, :], 2048)
            load(u0 + 1, 0, None, A["w_uq"][0, :, :], 1536)
            load(u0 + 2, 0, None, A["w_uq"][1, :, :], 1536)
            load(u0 + 3, 0, None, A["w_ukv"][1, :, :], 2048)
            with sp.Fori(0, 3) as r:
                for i in range(2):
                    load(u0 + 2 * i + 4, 4, r, A["w_uq"][ds(r * 2 + (i + 2), 1), :, :].rearrange("a p n -> p (a n)"), 1536)
                    load(u0 + 2 * i + 5, 4, r,
                         A["w_ukv"][ds(r * 2 + (i + 2), 1), :, :].rearrange("a p n -> p (a n)"), 2048)
            stream("w_oo", OO_P0, 16, 2048)
            feed_forward(1, F1_P0)

        def geometry(kind, p):
            if kind == "std":
                return 1024 * (p % 2), 1024
            if kind == "down":
                return 768 * (p % 2), (768, 640)[p % 2]
            if kind == "uq":
                return 768 * (p % 2), 768
            raise ValueError(kind)

        even_loads = sem("even_loads")
        bb_ready = sem("bb_ready")
        u_ready = sem("u_ready")
        c_ready = sem("c_ready")
        kx_ready = sem("kx_ready")
        bt_psum = sem("bt_psum")
        bt_ready = sem("bt_ready")
        kq_ready = sem("kq_ready")
        v_ready = sem("v_ready")
        s_done = sem("s_done")
        pm_ready = sem("pm_ready")
        o_done = sem("o_done")
        osq_ready = sem("osq_ready")
        osum_done = sem("osum_done")
        ovar_ready = sem("ovar_ready")
        osd_ready = sem("osd_ready")
        gs_ready = sem("gs_ready")
        yt_ready = sem("yt_ready")
        yh_ready = sem("yh_ready")
        yl_ready = sem("yl_ready")
        dec_in = sem("dec_in")
        cst_in = sem("cst_in")
        staged = sem("staged")
        cneg_ready = sem("cneg_ready")
        ku_ready = sem("ku_ready")
        den_ready = sem("den_ready")
        bu_done = sem("bu_done")
        bu_copied = sem("bu_copied")
        w_ready = sem("w_ready")
        z_ready = sem("z_ready")
        c_done = sem("c_done")
        y5_ready = sem("y5_ready")
        ge_ready = sem("ge_ready")
        gluw_in = sem("gluw_in")
        glu_done = sem("glu_done")
        glu_sig = sem("glu_sig")
        glu_mul = sem("glu_mul")
        glu_hi = sem("glu_hi")
        glu_lo = sem("glu_lo")

        conv_in = sem("conv_in")
        cws_ready = sem("cws_ready")
        cv_ready = sem("cv_ready")
        vc_ready = sem("vc_ready")
        silu_ready = sem("silu_ready")
        hid_ready = sem("hid_ready")
        hh_ready = sem("hh_ready")
        hl_ready = sem("hl_ready")

        odd_loads = sem("odd_loads")
        csq_ready = sem("csq_ready")
        csum_done = sem("csum_done")
        cvar_ready = sem("cvar_ready")
        csd_ready = sem("csd_ready")
        ct_ready = sem("ct_ready")
        ch_ready = sem("ch_ready")
        cl_ready = sem("cl_ready")
        sw_done = sem("sw_done")
        qa_copied = sem("qa_copied")
        qa_free = sem("qa_free")
        kb_copied = sem("kb_copied")
        kb_free = sem("kb_free")
        v2_ready = sem("v2_ready")
        kr_ready = sem("kr_ready")
        kx_copied = sem("kx_copied")
        qr_ready = sem("qr_ready")
        sc_done = sem("sc_done")
        sc_read = sem("sc_read")
        mx_ready = sem("mx_ready")
        ex_ready = sem("ex_ready")
        pn_ready = sem("pn_ready")
        pt_done = sem("pt_done")
        pt_ready = sem("pt_ready")
        at_done = sem("at_done")
        ah_ready = sem("ah_ready")
        al_ready = sem("al_ready")
        fin_ready = sem("fin_ready")
        stored = sem("stored")

        @block.scalar
        def _(act):
            def split(p, s, r, kind="std"):
                u = p // 2
                off, n = geometry(kind, p)
                act.wait_ge(raw_full[u % SLOTS], at(16 * (u // SLOTS + 1), 2 * s, r))
                if p >= SLOTS:
                    act.wait_ge(piece_done, at(p - SLOTS + 1, s, r))
                act.activation(hi[:, p % SLOTS, 0:n], raw[:, u % SLOTS, off:off + n], ACT.Copy).then_inc(hi_ready, 1)

            def splits(p, s=0, r=None, kinds=("std",) * 4):
                for i, k in enumerate(kinds):
                    split(p + i, s, r, k)

            def copy_low(p_end, e, sp_=0, se=0, r=None):
                act.wait_ge(piece_done, at(p_end, sp_, r))
                if e > 0:
                    act.wait_ge(bank_free, at(e, se, r))
                b = pair(e)
                act.activation(lot[:, :, :], PS[:, b:b + 2, T:2 * T], ACT.Copy).then_inc(lo_copied, 1)

            def square_quarter(c):
                act.wait_ge(x_in[c], 16)
                if c >= 2:
                    act.wait_ge(sq_added, c - 1)
                act.activation((sT1, sT2)[c % 2].rearrange("p a b t -> p (a b) t"), H[:, 4 * c:4 * c + 4, :],
                               ACT.Square).then_inc(sq_ready, 1)

            def round_x(n, j, s=0, r=None):
                act.wait_ge(xt_ready, at(8 * n + j + 1, s, r))
                x = XS[:, 2 * j:2 * j + 2, :] if r is None else XS[:, ds(r * (2 * s) + 2 * j, 2), :]
                act.activation(x[:, :, 0:T], txn[:, j % 2, :, :], ACT.Copy).then_inc(xh_ready, 1)

            def root(n):
                act.wait_ge(var_ready, n + 1)
                act.activation(nwt[:, 1, :], nwt[:, 0, :], ACT.Sqrt).then_inc(sd_ready, 1)

            def first_step(n, p):
                splits(p, kinds=("std",) * 2)
                root(n)
                splits(p + 2, kinds=("std",) * 2)

            act.dma_start(vec[:, :], A["vec"]).then_inc(small_in, 16)
            for c in range(4):
                round_x(0, 2 * c)
                round_x(0, 2 * c + 1)
                split(c, 0, None)
                square_quarter(c)
                if c == 1:
                    act.dma_start(ident[:, :], A["ident"]).then_inc(small_in, 16)
                    act.dma_start(sB[:, :, :, :].rearrange("p a b t -> p (a b t)"), A["s5b"]).then_inc(even_loads, 16)
                    act.dma_start(cosR[:, :], A["cosR"]).then_inc(even_loads, 16)
                    act.dma_start(sinR[:, :], A["sinR"]).then_inc(even_loads, 16)

            first_step(0, 4)
            copy_low(4, 0)
            splits(8)
            copy_low(8, 1)
            act.wait_ge(rt_done, 1)
            act.activation(rtok[:, :], PS[:, 7, T:T + 2], ACT.Copy).then_inc(rt_ready, 1)

            def even_head(r, h0, s5, glu=False):
                p0, e0 = 8 + 16 * h0, 2 + 4 * h0
                H_ = lambda c, s: at(c + s * h0, s, r)
                S_ = lambda c, s: at(c + s * (h0 - 1), s, r)

                def bu_copy(m):
                    act.wait_ge(bu_done, S_(m + 1, 4))
                    if m % 2 == 0 and h0 - 1 + m > 0:
                        act.wait_ge(z_ready, S_(m // 2, 2))
                    act.activation(sB[:, :, m % 2, :], PS[:, 7, :].rearrange("p (a t) -> p a t", a=2),
                                   ACT.Copy).then_inc(bu_copied, 1)
                if h0:
                    act.wait_ge(pm_ready, H_(0, 1))
                act.dma_start(dec[:, :], A["dec"][h0, :, :] if r is None else
                              A["dec"][ds(r + h0, 1), :, :].rearrange("a p n -> p (a n)")).then_inc(dec_in, 16)
                if s5:
                    if h0 > 1:
                        act.wait_ge(c_done, S_(0, 2))
                    act.dma_start(Cst[:, :, :, :].rearrange("p a b c -> p (a b c)"),
                                  A["s5c"][h0 - 1, :, :] if r is None else
                                  A["s5c"][ds(r + (h0 - 1), 1), :, :].rearrange("a p n -> p (a n)")).then_inc(cst_in, 16)
                if glu:
                    act.wait_ge(c_done, 8)
                    act.dma_start(gluw, A["gluw"]).then_inc(gluw_in, 16)
                for i in range(4):
                    if h0 == 0 or i:
                        split(p0 + 4 + i, 16, r)
                    if s5 and i == 1:
                        bu_copy(0)
                copy_low(p0 + 4, e0, 16, 4, r)
                if glu:
                    act.wait_ge(y5_ready, 4)
                    act.activation(U[:, :, :], U[:, :, :], ACT.Gelu_apprx_tanh).then_inc(ge_ready, 1)
                for i in range(4):
                    split(p0 + 8 + i, 16, r)
                    if s5 and i == 0:
                        bu_copy(1)
                copy_low(p0 + 8, e0 + 1, 16, 4, r)
                for i in range(4):
                    split(p0 + 12 + i, 16, r)
                    if s5 and i < 2:
                        bu_copy(i + 2)
                act.wait_ge(piece_done, at(p0 + 12, 16, r))
                act.wait_ge(bank_free, at(e0 + 2, 4, r))
                act.activation(Vr[:, 0, :], PS[:, pair(e0 + 2), 0:T], ACT.Copy, scale=rtok[:, 0:1]).then_inc(lo_copied, 1)
                if glu:
                    act.wait_ge(small_in, 32)
                    act.wait_ge(glu_done, 4)
                    for t in range(KR):
                        ins = act.activation(sigs[:, t, :], PS[:, 6 + t // 2, (t % 2) * T:(t % 2 + 1) * T], ACT.Sigmoid,
                                             bias=vec[:, VEC["glub"] + t:VEC["glub"] + t + 1])
                    ins.then_inc(glu_sig, 1)
                act.wait_ge(o_done, H_(1, 1))
                act.activation(sq[:, :, :], PS[:, 5, :].rearrange("p (a t) -> p a t", a=2), ACT.Square).then_inc(osq_ready, 1)
                for i in range(4):
                    split(p0 + 16 + i, 16, r)
                    if glu and i == 1:
                        act.wait_ge(glu_mul, 1)
                        act.activation(Y5[:, :, 0:T], sigs, ACT.Copy).then_inc(glu_hi, 1)
                    if h0 == 0 and i == 2:
                        act.wait_ge(bt_psum, 8)
                        for b in range(2):
                            act.activation(BT[:, 2 * b:2 * b + 2, :, :].rearrange("p a b c -> p (a b c)"),
                                           PS[:, 6 + b, :], ACT.Copy).then_inc(bt_ready, 1)
                copy_low(p0 + 16, e0 + 3, 16, 4, r)
                act.wait_ge(ovar_ready, H_(1, 1))
                act.activation(nwt[:, 1, :], nwt[:, 0, :], ACT.Sqrt).then_inc(osd_ready, 1)
                act.wait_ge(ku_ready, H_(1, 1))
                act.activation(kq[:, :, :], Gr[:, :, :], ACT.Silu).then_inc(gs_ready, 1)
                if not glu:
                    split(p0 + 20, 16, r)
                act.wait_ge(yt_ready, H_(1, 1))
                dsty = YE[:, 2 * h0:2 * h0 + 2, 0:T] if r is None else YE[:, ds(r * 2 + 2 * h0, 2), 0:T]
                act.activation(dsty, txn[:, 0, :, :], ACT.Copy).then_inc(yh_ready, 1)

            even_head(None, 0, False)
            even_head(None, 1, True)
            with act.Fori(0, 3) as r:
                even_head(r, 2, True)
            even_head(None, 5, False, True)

            def out_projection(n, p0):
                with act.Fori(0, 3) as r:
                    for i in range(2):
                        splits(p0 + 4 * i + 4, 8, r)
                        round_x(n, i, 2, r)
                splits(p0 + 28)
                round_x(n, 6)
                splits(p0 + 32, kinds=("std",) * 3)
                round_x(n, 7)
                split(p0 + 35, 0, None)

            def feed_forward(layer, n, p0, e0):
                for half in range(2):
                    p = p0 + half * (UPP + DNP)
                    e = e0 + half * (2 * GS + 8)
                    s0 = (2 * layer + half) * GS

                    def up(r, j0, kinds, first, last=False):
                        q = p + 8 * j0
                        if first:
                            first_step(n, q + 4)
                        else:
                            splits(q + 4, 8, r)
                        copy_low(q + 4, e + 2 * j0, 8, 2, r)
                        splits(q + 8, 8, r, kinds)
                        copy_low(q + 8, e + 2 * j0 + 1, 8, 2, r)
                        act.wait_ge(cws_ready, at(s0 + j0 + 1, 1, r))
                        act.wait_ge(a_ready, at(s0 + j0 + 1, 1, r))
                        for t in range(2):
                            ins = act.activation(cvo[:, 1, t, :], apad[:, 1, t, 2:T + 2], ACT.Identity,
                                                 bias=cws[:, 4 * t + 11:4 * t + 12], scale=cws[:, 4 * t + 10:4 * t + 11])
                        ins.then_inc(vc_ready, 1)
                        if last:
                            split(q + 12, 0, None, "down")
                        act.wait_ge(cv_ready, at(s0 + j0 + 1, 1, r))
                        if s0 + j0:
                            act.wait_ge(hid_ready, at(s0 + j0, 1, r))
                        act.activation(sg[:, :, :], cvo[:, 0, :, :], ACT.Silu).then_inc(silu_ready, 1)
                        if last:
                            split(q + 13, 0, None, "down")
                        act.wait_ge(hid_ready, at(s0 + j0 + 1, 1, r))
                        if r is None:
                            dh = YF[:, 2 * j0:2 * j0 + 2, 0:T]
                        else:
                            dh = YF[:, ds(r * 2 + 2 * j0, 2), 0:T]
                        act.activation(dh, hid[:, :, :], ACT.Copy).then_inc(hh_ready, 1)

                    up(None, 0, ("std",) * 4, half == 0)
                    with act.Fori(0, GS - 2) as r:
                        up(r, 1, ("std",) * 4, False)
                    up(None, GS - 1, ("down",) * 4, False, True)
                    q = p + UPP
                    splits(q + 6, kinds=("down",) * 6)
                    if half == 1 and n < 3:
                        round_x(n + 1, 0)
                    with act.Fori(0, 3) as r:
                        for i in (1, 2):
                            splits(q + 8 * i + 4, 16, r, ("down",) * 8)
                            if half == 1 and n < 3:
                                round_x(n + 1, i, 2, r)
                    splits(q + 60, kinds=("down",) * 4)
                    if half == 0:
                        splits(q + 64)
                    elif n < 3:
                        splits(q + 64, kinds=("std",) * 3)
                        round_x(n + 1, 7)
                        split(q + 67, 0, None)

            out_projection(1, OE_P0)
            act.wait_ge(piece_done, F0_P0)
            act.wait_ge(bank_free, F0_E0)
            act.dma_start(cw[:, :, :], A["conv"][0, :, :, :]).then_inc(conv_in, 16)
            feed_forward(0, 1, F0_P0, F0_E0)
            act.wait_ge(piece_done, MD_P0)
            act.wait_ge(bank_free, MD_E0)
            act.dma_start(caus[:, :], A["caus"]).then_inc(odd_loads, 16)
            act.dma_start(mcos[:, :], A["mcos"]).then_inc(odd_loads, 16)
            act.dma_start(msin[:, :], A["msin"]).then_inc(odd_loads, 16)
            act.dma_start(swp[:, :], A["swp"]).then_inc(odd_loads, 16)

            def csquare(j):
                act.wait_ge(c_ready, j + 1)
                if j >= 2:
                    act.wait_ge(csum_done, j - 1)
                act.activation(txn[:, j % 2, :, :], C8[:, 2 * j:2 * j + 2, :], ACT.Square).then_inc(csq_ready, 1)

            def croot(w):
                act.wait_ge(cvar_ready, w + 1)
                act.activation(nwt[:, 1, :], nwt[:, 0, :], ACT.Sqrt).then_inc(csd_ready, 1)

            def round_c(j):
                act.wait_ge(ct_ready, j + 1)
                act.activation(CS[:, 2 * j:2 * j + 2, 0:T], cn[:, j % 2, :, :], ACT.Copy).then_inc(ch_ready, 1)

            q = MD_P0
            splits(q + 4, kinds=("std",) * 2)
            root(2)
            copy_low(q + 2, MD_E0)
            splits(q + 6)
            copy_low(q + 6, MD_E0 + 1)
            csquare(0)
            splits(q + 10)
            copy_low(q + 10, MD_E0 + 2)
            csquare(1)
            splits(q + 14, kinds=("std",) * 3)
            croot(0)
            split(q + 17, 0, None)
            copy_low(q + 14, MD_E0 + 3)
            csquare(2)
            split(q + 18, 0, None)
            round_c(0)
            round_c(1)
            split(q + 19, 0, None)
            round_c(2)
            split(q + 20, 0, None, "uq")
            copy_low(q + 18, MD_E0 + 4)
            csquare(3)
            round_c(3)
            split(q + 21, 0, None, "uq")

            def exponentials(r, c0):
                for h in range(2):
                    act.wait_ge(mx_ready, at(2 * c0 + h + 1, 4, r))
                    act.activation(Sc[:, h, 0:P], Sc[:, h, 0:P], ACT.Exp, bias=st8[:, h, 0:1],
                                   accum_out=st8[:, h, 2:3])
                    act.activation(Sc[:, h, P:3 * P], Sc[:, h, P:3 * P], ACT.Exp, bias=st8[:, h, 1:2],
                                   accum_out=st8[:, h, 3:4]).then_inc(ex_ready, 1)

            def attended(r, c0):
                for h in range(2):
                    act.wait_ge(pt_done, at(2 * c0 + h + 1, 4, r))
                    act.activation(PT[:, h, :], PS[:, 6 + h, 0:3 * P], ACT.Copy).then_inc(pt_ready, 1)
                act.wait_ge(at_done, at(c0 + 1, 2, r))
                dy = YO[:, 2 * c0:2 * c0 + 2, 0:T] if r is None else YO[:, ds(r * 4 + 2 * c0, 2), 0:T]
                act.activation(dy, PS[:, 3, :].rearrange("p (a t) -> p a t", a=2), ACT.Copy).then_inc(ah_ready, 1)

            def copy_values():
                act.activation(V2[:, :, :], PS[:, 5, :].rearrange("p (a t) -> p a t", a=2),
                               ACT.Copy).then_inc(v2_ready, 1)

            def pair_body(r, c0, last=False):
                p0 = MP_P0 + 4 * c0
                splits(p0 + 2, 8, r, ("std",) * 2)
                act.wait_ge(piece_done, at(p0 + 2, 8, r))
                act.wait_ge(qa_free, at(c0, 2, r))
                act.activation(lo4[:, 0:3, :], PS[:, 0:3, T:2 * T], ACT.Copy).then_inc(qa_copied, 1)
                exponentials(r, c0 - 1)
                splits(p0 + 4, 8, r, ("std", "std") if last else ("uq", "uq"))
                act.wait_ge(piece_done, at(p0 + 4, 8, r))
                act.wait_ge(kb_free, at(c0, 2, r))
                act.activation(lo4[:, 3:5, :], PS[:, 3:5, T:2 * T], ACT.Copy).then_inc(kb_copied, 1)
                attended(r, c0 - 1)
                copy_values()

            act.wait_ge(piece_done, MP_P0 + 2)
            act.activation(lo4[:, 3:5, :], PS[:, 3:5, T:2 * T], ACT.Copy).then_inc(kb_copied, 1)
            copy_values()
            croot(1)
            splits(MP_P0 + 4, kinds=("uq", "uq"))
            act.wait_ge(piece_done, MP_P0 + 4)
            act.activation(lo4[:, 0:3, :], PS[:, 0:3, T:2 * T], ACT.Copy).then_inc(qa_copied, 1)
            with act.Fori(0, 3) as r:
                pair_body(r, 1)
                pair_body(r, 2)
            pair_body(None, 7, True)
            splits(OO_P0 + 2, kinds=("std",) * 2)
            exponentials(None, 7)
            attended(None, 7)

            out_projection(3, OO_P0)
            act.wait_ge(piece_done, F1_P0)
            act.wait_ge(bank_free, F1_E0)
            act.dma_start(cw[:, :, :], A["conv"][1, :, :, :]).then_inc(conv_in, 16)
            feed_forward(1, 3, F1_P0, F1_E0)
            root(4)
            for k in range(8):
                j = (0, 5, 1, 2, 6, 3, 4, 7)[k]
                if j < FINAL_DVE:
                    act.wait_ge(fin_ready, j + 1)
                else:
                    act.wait_ge(fin_pool, j - FINAL_DVE + 1)
                act.dma_start(out[:, 2 * j:2 * j + 2, :], H[:, 2 * j:2 * j + 2, :]).then_inc(stored, 16)
            act.wait_ge(stored, 16 * 8)

        @block.vector
        def _(dve):
            V = nc.vector

            def split(p, s, r, kind="std"):
                u = p // 2
                off, n = geometry(kind, p)
                dve.wait_ge(hi_ready, at(p + 1, s, r))
                V.tensor_tensor(lo[:, p % SLOTS, 0:n], raw[:, u % SLOTS, off:off + n], f(hi[:, p % SLOTS, 0:n]),
                                ALU.subtract).then_inc(lo_ready, 1)

            def splits(p, s=0, r=None, kinds=("std",) * 4):
                for i, k in enumerate(kinds):
                    split(p + i, s, r, k)

            def add_banks(dstap, e, se=0, r=None, l=None):
                dve.wait_ge(lo_copied, at((e if l is None else l) + 1, se, r))
                b = pair(e)
                return V.tensor_tensor(dstap, PS[:, b:b + 2, 0:T], lot[:, :, :], ALU.add)

            def add_residual(p_end, e, sp_, se, r, j0, n=None):
                dve.wait_ge(piece_done, at(p_end, sp_, r))
                b = pair(e)
                h = H[:, 2 * j0:2 * j0 + 2, :] if r is None else H[:, ds(r * 4 + 2 * j0, 2), :]
                V.tensor_tensor(h, h, PS[:, b:b + 2, 0:T], ALU.add)
                dve.drain()
                V.tensor_tensor(h, h, PS[:, b:b + 2, T:2 * T], ALU.add).then_inc(bank_free, 1)
                if n == 4:
                    dve.drain()
                    if r is None and j0 == 7:
                        V.tensor_tensor(lot[:, :, :], h, h, ALU.mult).then_inc(last_sq, 1)
                    for t in range(2):
                        c = VEC["g_fin"] + 2 * j0 + t
                        ht, g, k = ((H[:, 2 * j0 + t, :], vec[:, c:c + 1], XF[:, 2 * j0 + t, :]) if r is None else
                                    (H[:, ds(r * 4 + (2 * j0 + t), 1), :].rearrange("p a t -> p (a t)"),
                                     vec[:, ds(r * 4 + c, 1)],
                                     XF[:, ds(r * 4 + (2 * j0 + t), 1), :].rearrange("p a t -> p (a t)")))
                        V.tensor_scalar(k, ht, g, None, ALU.mult)
                elif n is not None:
                    dve.drain()
                    x_pair(n, j0, r)
                    x_low(n, j0, r)

            def x_pair(n, j, r=None):
                c = (VEC["g_even"], VEC["g_ffn"], VEC["g_odd"], VEC["g_ffn"] + KD)[n] + 2 * j
                for t in range(2):
                    if r is None:
                        h, g = H[:, 2 * j + t, :], vec[:, c + t:c + t + 1]
                    else:
                        h, g = H[:, ds(r * 4 + (2 * j + t), 1), :].rearrange("p a t -> p (a t)"), vec[:, ds(r * 4 + (c + t), 1)]
                    ins = V.tensor_scalar(txn[:, j % 2, t, :], h, g, None, ALU.mult)
                ins.then_inc(xt_ready, 1)

            def x_low(n, j, r=None):
                dve.wait_ge(xh_ready, at(8 * n + j + 1, 2, r))
                x = XS[:, 2 * j:2 * j + 2, :] if r is None else XS[:, ds(r * 4 + 2 * j, 2), :]
                V.tensor_tensor(x[:, :, T:2 * T], txn[:, j % 2, :, :], f(x[:, :, 0:T]), ALU.subtract).then_inc(xl_ready, 1)

            rn2 = rn[:, :].unsqueeze(1).broadcast_to([P, 2, T])

            def add_scaled(d, e, se=0, r=None, l=None):
                add_banks(d, e, se, r, l).then_inc(bank_free, 1)
                dve.drain()
                return V.tensor_tensor(d, d, rn2, ALU.mult)

            def inv_rms(psum, width, var_sem, sd_sem, count, out_=rn[:, :], tmp=nwt[:, 2, :]):
                V.tensor_scalar(nwt[:, 0, :], psum, 1.0 / width, EPS, ALU.mult, ALU.add).then_inc(var_sem, 1)
                dve.wait_ge(sd_sem, count)
                V.reciprocal(out_, nwt[:, 1, :])
                dve.drain()
                V.tensor_tensor(tmp, out_, out_, ALU.mult)
                dve.drain()
                V.scalar_tensor_tensor(out=tmp, in0=tmp, scalar=-0.5, in1=nwt[:, 0, :], op0=ALU.mult, op1=ALU.mult)
                dve.drain()
                V.scalar_tensor_tensor(out=out_, in0=tmp, scalar=1.5, in1=out_, op0=ALU.add, op1=ALU.mult)
                dve.drain()

            def root(n):
                dve.wait_ge(sum_done, n + 1)
                inv_rms(PS[:, 7, 0:T], D, var_ready, sd_ready, n + 1)

            def first_step(n, p):
                splits(p, kinds=("std",) * 2)
                root(n)
                splits(p + 2, kinds=("std",) * 2)

            def lambda_squared():
                lre, lim = (vec[:, VEC[k]:VEC[k] + KD] for k in ("lre", "lim"))
                V.tensor_tensor(pt[:, 12, :], lre, lre, ALU.mult)
                V.tensor_tensor(pt[:, 13, :], lim, lim, ALU.mult)
                dve.drain()
                V.tensor_tensor(pt[:, 13, :], pt[:, 12, :], pt[:, 13, :], ALU.add)
                dve.drain()
                V.reciprocal(pt[:, 12, :], pt[:, 13, :]).then_inc(den_ready, 1)

            V.memset(ones[:, :], 1.0).then_inc(ones_set, 1)
            dve.wait_ge(small_in, 16)
            for c in range(4):
                dve.wait_ge(x_in[c], 16)
                dve.drain()
                x_pair(0, 2 * c)
                x_pair(0, 2 * c + 1)
                x_low(0, 2 * c)
                x_low(0, 2 * c + 1)
                split(c, 0, None)
                if c == 0:
                    lambda_squared()
            first_step(0, 4)
            add_scaled(U[:, 0:2, :], 0)
            splits(8)
            add_scaled(U[:, 2:4, :], 1).then_inc(u_ready, 1)
            dve.wait_ge(even_loads, 48)

            def even_head(r, h0, s5, glu=False):
                p0, e0 = 8 + 16 * h0, 2 + 4 * h0
                H_ = lambda c, s: at(c + s * h0, s, r)
                S_ = lambda c, s: at(c + s * (h0 - 1), s, r)

                def rotate(d, e):
                    add_scaled(kq[:, :, :], e, 4, r)
                    dve.drain()
                    ra, rb = txn[:, 0], txn[:, 1]
                    V.tensor_tensor(ra, kq[:, :, :], cosR[:, :].unsqueeze(1).broadcast_to([P, 2, T]), ALU.mult)
                    V.tensor_tensor(rb, kq[:, :, :], sinR[:, :].unsqueeze(1).broadcast_to([P, 2, T]), ALU.mult)
                    dve.drain()
                    V.tensor_tensor(d[:, 0, :], ra[:, 0], rb[:, 1], ALU.subtract)
                    V.tensor_tensor(d[:, 1, :], ra[:, 1], rb[:, 0], ALU.add).then_inc(kq_ready, 1)

                def scan(k):
                    dve.wait_ge(w_ready, S_(k + 1, 2))
                    for ri in range(2):
                        for m in range(2):
                            V.tensor_tensor_scan(sT1[:, ri, m, :], magst[:, m:m + 1].broadcast_to([P, T]),
                                                 sB[:, ri, m, :], 0.0, ALU.mult, ALU.add)
                    dve.drain()
                    eb = E[:, k]
                    V.tensor_tensor(sT2, sT1, eb[:, 0:1].broadcast_to([P, 2, 2, T]), ALU.mult)
                    V.tensor_tensor(sB, sT1, eb[:, 1:2].broadcast_to([P, 2, 2, T]), ALU.mult)
                    dve.drain()
                    V.tensor_tensor(sT1[:, 0], sT2[:, 0], sB[:, 1], ALU.subtract)
                    V.tensor_tensor(sT1[:, 1], sT2[:, 1], sB[:, 0], ALU.add).then_inc(z_ready, 1)

                for i in range(4):
                    if h0 == 0 or i:
                        split(p0 + 4 + i, 16, r)
                rotate(KRo, e0)
                for i in range(4):
                    split(p0 + 8 + i, 16, r)
                    if s5 and i == 1:
                        scan(0)
                rotate(QRo, e0 + 1)
                splits(p0 + 12, 16, r)
                dve.wait_ge(lo_copied, at(e0 + 3, 4, r))
                V.tensor_scalar(Vr[:, 1, :], PS[:, pair(e0 + 2) + 1, 0:T], rtok[:, 1:2], None, ALU.mult).then_inc(bank_free, 1)
                dve.wait_ge(s_done, H_(1, 1))
                dve.wait_ge(dec_in, H_(16, 16))
                V.tensor_tensor(Pm[:, 0:T], PS[:, 4, 0:T], dec[:, :], ALU.mult)
                V.tensor_tensor(Pm[:, T:T + P], PS[:, 4, T:T + P], dec[:, 0:P], ALU.mult).then_inc(pm_ready, 1)
                if s5:
                    scan(1)
                if glu:
                    dve.wait_ge(glu_sig, 1)
                    V.tensor_tensor(sigs, sigs, U[:, :, :], ALU.mult).then_inc(glu_mul, 1)
                for i in range(4):
                    split(p0 + 16 + i, 16, r)
                    if glu and i == 1:
                        dve.wait_ge(glu_hi, 1)
                        V.tensor_tensor(Y5[:, :, T:2 * T], sigs, f(Y5[:, :, 0:T]), ALU.subtract).then_inc(glu_lo, 1)
                add_scaled(Gr[:, :, :], e0 + 3, 4, r).then_inc(ku_ready, 1)
                dve.wait_ge(osum_done, H_(1, 1))
                norm_head(H_(1, 1))
                if not glu:
                    split(p0 + 20, 16, r)
                for t in range(2):
                    c = VEC["ret"] + 2 * h0 + t
                    wcol = vec[:, c:c + 1] if r is None else vec[:, ds(r * 2 + c, 1)]
                    V.scalar_tensor_tensor(out=txn[:, 0, t, :], in0=PS[:, 5, t * T:(t + 1) * T], scalar=wcol,
                                           in1=ro, op0=ALU.mult, op1=ALU.mult)
                dve.drain()
                dve.wait_ge(gs_ready, H_(1, 1))
                V.tensor_tensor(txn[:, 0, :, :], txn[:, 0, :, :], kq[:, :, :], ALU.mult).then_inc(yt_ready, 1)
                if s5:
                    dve.wait_ge(c_done, S_(2, 2))
                    k = h0 - 1
                    u = U[:, k, :] if r is None else U[:, ds(r + k, 1), :].rearrange("p a t -> p (a t)")
                    c = VEC["d"] + k
                    V.scalar_tensor_tensor(out=u, in0=u, scalar=vec[:, c:c + 1] if r is None else vec[:, ds(r + c, 1)],
                                           in1=PS[:, 6, 0:T], op0=ALU.mult, op1=ALU.add).then_inc(y5_ready, 1)
                dve.wait_ge(yh_ready, H_(1, 1))
                ye = YE[:, 2 * h0:2 * h0 + 2, :] if r is None else YE[:, ds(r * 2 + 2 * h0, 2), :]
                V.tensor_tensor(ye[:, :, T:2 * T], txn[:, 0, :, :], f(ye[:, :, 0:T]), ALU.subtract).then_inc(yl_ready, 1)

            ro = nwt[:, 2, :]

            def norm_head(count):
                inv_rms(PS[:, 4, 0:T], RD, ovar_ready, osd_ready, count, out_=ro, tmp=sq[:, 0, :])

            dve.wait_ge(rt_ready, 1)
            even_head(None, 0, False)
            even_head(None, 1, True)
            with dve.Fori(0, 3) as r:
                even_head(r, 2, True)
            even_head(None, 5, False, True)

            def out_projection(n, p0, e0):
                with dve.Fori(0, 3) as r:
                    for i in range(2):
                        splits(p0 + 4 * i + 4, 8, r)
                        add_residual(p0 + 4 * i + 4, e0 + i, 8, 2, r, i, n)
                splits(p0 + 28)
                add_residual(p0 + 28, e0 + 6, 0, 0, None, 6, n)
                splits(p0 + 32, kinds=("std",) * 3)
                add_residual(p0 + 32, e0 + 7, 0, 0, None, 7, n)
                split(p0 + 35, 0, None)

            def feed_forward(layer, n, p0, e0, l0):
                for half in range(2):
                    p = p0 + half * (UPP + DNP)
                    e = e0 + half * (2 * GS + 8)
                    l = l0 + half * 2 * GS
                    s0 = (2 * layer + half) * GS

                    def up(r, j0, kinds, first, last=False):
                        q = p + 8 * j0
                        if first:
                            first_step(n, q + 4)
                            dve.sem_inc(rn_ready, 1)
                        else:
                            splits(q + 4, 8, r)
                        if s0 + j0:
                            dve.wait_ge(cv_ready, at(s0 + j0, 1, r))
                        add_banks(apad[:, 0, :, 2:T + 2], e + 2 * j0, 2, r, l + 2 * j0).then_inc(bank_free, 1)
                        splits(q + 8, 8, r, kinds)
                        add_scaled(apad[:, 1, :, 2:T + 2], e + 2 * j0 + 1, 2, r, l + 2 * j0 + 1).then_inc(a_ready, 1)
                        if last:
                            split(q + 12, 0, None, "down")
                        dve.wait_ge(vc_ready, at(s0 + j0 + 1, 1, r))
                        for i in (1, 0):
                            for t in range(2):
                                V.scalar_tensor_tensor(out=cvo[:, 1, t, :], in0=apad[:, 1, t, i:T + i],
                                                       scalar=cws[:, 8 + 4 * t + i:9 + 4 * t + i], in1=cvo[:, 1, t, :],
                                                       op0=ALU.mult, op1=ALU.add)
                            dve.drain()
                        dve.wait_ge(silu_ready, at(s0 + j0 + 1, 1, r))
                        V.tensor_tensor(hid[:, :, :], sg[:, :, :], cvo[:, 1, :, :], ALU.mult).then_inc(hid_ready, 1)
                        if last:
                            split(q + 13, 0, None, "down")
                        dve.wait_ge(hh_ready, at(s0 + j0 + 1, 1, r))
                        if r is None:
                            y = YF[:, 2 * j0:2 * j0 + 2, :]
                        else:
                            y = YF[:, ds(r * 2 + 2 * j0, 2), :]
                        V.tensor_tensor(y[:, :, T:2 * T], hid[:, :, :], f(y[:, :, 0:T]), ALU.subtract).then_inc(hl_ready, 1)

                    up(None, 0, ("std",) * 4, half == 0)
                    with dve.Fori(0, GS - 2) as r:
                        up(r, 1, ("std",) * 4, False)
                    up(None, GS - 1, ("down",) * 4, False, True)
                    q = p + UPP
                    ed = e + 2 * GS
                    m = n + 1 if half == 1 else None
                    splits(q + 6, kinds=("down",) * 6)
                    add_residual(q + 8, ed, 0, 0, None, 0, m)
                    with dve.Fori(0, 3) as r:
                        for i in (1, 2):
                            splits(q + 8 * i + 4, 16, r, ("down",) * 8)
                            add_residual(q + 8 * i + 8, ed + i, 16, 2, r, i, m)
                    splits(q + 60, kinds=("down",) * 4)
                    if half == 0:
                        splits(q + 64)
                    elif n < 3:
                        splits(q + 64, kinds=("std",) * 3)
                    add_residual(q + 64, ed + 7, 0, 0, None, 7, m)
                    if half == 1 and n < 3:
                        split(q + 67, 0, None)

            out_projection(1, OE_P0, OE_E0)
            V.memset(apad[:, :, :, 0:2], 0.0)
            feed_forward(0, 1, F0_P0, F0_E0, F0_L0)

            def cnorm(w):
                dve.wait_ge(csum_done, 2 * w + 2)
                inv_rms(PS[:, 6 + w, 0:T], RANK, cvar_ready, csd_ready, w + 1, out_=rc[:, :])

            def c_pair(j):
                g = VEC[("kvn", "qn")[j // 2]] + 2 * (j % 2)
                for t in range(2):
                    o, x, w = cn[:, j % 2, t, :], C8[:, 2 * j + t, :], vec[:, g + t:g + t + 1]
                    if j < 2:
                        ins = V.scalar_tensor_tensor(out=o, in0=x, scalar=w, in1=rc[:, :], op0=ALU.mult, op1=ALU.mult)
                    else:
                        ins = V.tensor_scalar(o, x, w, None, ALU.mult)
                ins.then_inc(ct_ready, 1)

            def c_low(j):
                dve.wait_ge(ch_ready, j + 1)
                V.tensor_tensor(CS[:, 2 * j:2 * j + 2, T:2 * T], cn[:, j % 2, :, :], f(CS[:, 2 * j:2 * j + 2, 0:T]),
                                ALU.subtract).then_inc(cl_ready, 1)

            def rotary(dst_, x, bank, swapped):
                dve.drain()
                V.tensor_tensor(rt[:, 0, :], x, mcos[:, :], ALU.mult)
                dve.wait_ge(sw_done, swapped)
                V.tensor_tensor(rt[:, 1, :], PS[:, bank, 0:T], msin[:, :], ALU.mult)
                dve.drain()
                V.tensor_tensor(dst_, rt[:, 0, :], rt[:, 1, :], ALU.add).then_inc(qr_ready, 1)

            def c_banks(j):
                add_scaled(C8[:, 2 * j:2 * j + 2, :], MD_E0 + 1 + j, l=MD_L0 + 1 + j).then_inc(c_ready, 1)

            q = MD_P0
            splits(q + 4, kinds=("std",) * 2)
            root(2)
            dve.wait_ge(lo_copied, MD_L0 + 1)
            V.tensor_tensor(KX[:, :], PS[:, pair(MD_E0), 0:T], lot[:, 0, :], ALU.add).then_inc(bank_free, 1)
            dve.drain()
            V.tensor_tensor(KX[:, :], KX[:, :], rn[:, :], ALU.mult).then_inc(kx_ready, 1)
            splits(q + 6)
            c_banks(0)
            splits(q + 10)
            c_banks(1)
            dve.wait_ge(odd_loads, 64)
            rotary(KRp[:, :], KX[:, :], 5, 1)
            splits(q + 14, kinds=("std",) * 3)
            cnorm(0)
            split(q + 17, 0, None)
            c_banks(2)
            c_pair(0)
            c_pair(1)
            split(q + 18, 0, None)
            c_low(0)
            c_low(1)
            split(q + 19, 0, None)
            dve.drain()
            c_pair(2)
            c_low(2)
            split(q + 20, 0, None, "uq")
            c_banks(3)
            dve.drain()
            c_pair(3)
            c_low(3)
            split(q + 21, 0, None, "uq")

            def masked_scores(r, c0):
                for h in range(2):
                    dve.wait_ge(sc_done, at(2 * c0 + h + 1, 4, r))
                    if c0:
                        dve.wait_ge(pt_done, at(2 * c0 + h - 1, 4, r))
                    V.scalar_tensor_tensor(out=Sc[:, h, :], in0=PS[:, 6 + h, 0:3 * P], scalar=(MN + MR) ** -0.5,
                                           in1=caus[:, :], op0=ALU.mult, op1=ALU.add)
                    dve.drain()
                    V.tensor_reduce(st8[:, h, 0:1], Sc[:, h, 0:P], AX.X, ALU.max, negate=True)
                    V.tensor_reduce(st8[:, h, 1:2], Sc[:, h, P:3 * P], AX.X, ALU.max, negate=True).then_inc(mx_ready, 1)

            def probabilities(r, c0):
                for h in range(2):
                    dve.wait_ge(ex_ready, at(2 * c0 + h + 1, 4, r))
                    V.reciprocal(st8[:, h, 4:6], st8[:, h, 2:4])
                    dve.drain()
                    V.tensor_scalar(Sc[:, h, 0:P], Sc[:, h, 0:P], st8[:, h, 4:5], None, ALU.mult)
                    V.tensor_scalar(Sc[:, h, P:3 * P], Sc[:, h, P:3 * P], st8[:, h, 5:6], None, ALU.mult)\
                        .then_inc(pn_ready, 1)

            def attended_low(r, c0):
                dve.wait_ge(ah_ready, at(c0 + 1, 2, r))
                y = YO[:, 2 * c0:2 * c0 + 2, :] if r is None else YO[:, ds(r * 4 + 2 * c0, 2), :]
                V.tensor_tensor(y[:, :, T:2 * T], PS[:, 3, :].rearrange("p (a t) -> p a t", a=2), f(y[:, :, 0:T]),
                                ALU.subtract).then_inc(al_ready, 1)

            rc2 = rc[:, :].unsqueeze(1).broadcast_to([P, 2, T])

            def keys(r, c0):
                dve.wait_ge(kb_copied, at(c0 + 1, 2, r))
                V.tensor_tensor(KN[:, :, :], PS[:, 3:5, 0:T], lo4[:, 3:5, :], ALU.add).then_inc(kb_free, 1)

            def queries(r, c0):
                dve.wait_ge(qa_copied, at(c0 + 1, 2, r))
                V.tensor_tensor(QN[:, :, :], PS[:, 0:2, 0:T], lo4[:, 0:2, :], ALU.add)
                V.tensor_tensor(QX[:, :], PS[:, 2, 0:T], lo4[:, 2, :], ALU.add).then_inc(qa_free, 1)
                dve.drain()
                V.tensor_tensor(QN[:, :, :], QN[:, :, :], rc2, ALU.mult)

            def pair_body(r, c0, last=False):
                p0 = MP_P0 + 4 * c0
                splits(p0 + 2, 8, r, ("std",) * 2)
                masked_scores(r, c0 - 1)
                queries(r, c0)
                probabilities(r, c0 - 1)
                splits(p0 + 4, 8, r, ("std", "std") if last else ("uq", "uq"))
                keys(r, c0)
                rotary(QRp[:, :], QX[:, :], 2, at(c0 + 2, 2, r))
                attended_low(r, c0 - 1)

            keys(None, 0)
            cnorm(1)
            V.tensor_tensor(mcos[:, :], mcos[:, :], rc[:, :], ALU.mult)
            V.tensor_tensor(msin[:, :], msin[:, :], rc[:, :], ALU.mult)
            queries(None, 0)
            splits(MP_P0 + 4, kinds=("uq", "uq"))
            rotary(QRp[:, :], QX[:, :], 2, 2)
            with dve.Fori(0, 3) as r:
                pair_body(r, 1)
                pair_body(r, 2)
            pair_body(None, 7, True)
            splits(OO_P0 + 2, kinds=("std",) * 2)
            masked_scores(None, 7)
            probabilities(None, 7)
            attended_low(None, 7)

            out_projection(3, OO_P0, OO_E0)
            V.memset(apad[:, :, :, 0:2], 0.0)
            feed_forward(1, 3, F1_P0, F1_E0, F1_L0)

            dve.wait_ge(sum_done, 5)
            inv_rms(PS[:, 7, 0:T], D, var_ready, sd_ready, 5)
            dve.sem_inc(rn_ready, 1)
            for j in range(FINAL_DVE):
                V.tensor_tensor(H[:, 2 * j:2 * j + 2, :], XF[:, 2 * j:2 * j + 2, :], rnb, ALU.mult).then_inc(fin_ready, 1)

        @block.gpsimd
        def _(pool):
            G = nc.gpsimd

            def sum_squares(n, e, pairs=KD // 2):
                pool.wait_ge(sum_done, n)
                G.memset(acc[:, :, :], 0.0)
                with pool.Fori(0, pairs) as r:
                    pool.drain()
                    pool.wait_ge(bank_free, r + (e + 1))
                    h = H[:, ds(r * 2, 2), :]
                    G.tensor_tensor(sq[:, :, :], h, h, ALU.mult)
                    pool.drain()
                    G.tensor_tensor(acc[:, :, :], acc[:, :, :], sq[:, :, :], ALU.add)
                pool.drain()
                G.memset(mark[:, :], 0.0).then_inc(ssq_ready, 1)

            G.memset(acc[:, :, :], 0.0)
            for c in range(4):
                for i in range(2):
                    pool.drain()
                    if i == 0:
                        pool.wait_ge(sq_ready, c + 1)
                    ins = G.tensor_tensor(acc[:, :, :], acc[:, :, :], (sT1, sT2)[c % 2][:, i], ALU.add)
                ins.then_inc(sq_added, 1)

            def s5_setup():
                lre, lim, ldt = (vec[:, VEC[k]:VEC[k] + KD] for k in ("lre", "lim", "ldt"))
                col = lambda i: pt[:, i, :]

                def tt(o, a, b, op):
                    G.tensor_tensor(o, a, b, op)
                    pool.drain()

                def ts(o, a, s1, s2, o1, o2=None):
                    if o2 is None:
                        G.tensor_scalar(o, a, s1, None, o1)
                    else:
                        G.tensor_scalar(o, a, s1, s2, o1, o2)
                    pool.drain()

                def stt(o, a, s, b, o1, o2):
                    ts(col(14), a, s, None, o1)
                    tt(o, col(14), b, o2)

                MAGIC = 12582912.0

                def exp(o, z, a, b, c):
                    ts(o, z, -150.0, 130.0, ALU.max, ALU.min)
                    ts(a, o, 1.4426950408889634, MAGIC, ALU.mult, ALU.add)
                    ts(a, a, -MAGIC, None, ALU.add)
                    stt(b, a, -0.693359375, o, ALU.mult, ALU.add)
                    stt(b, a, 2.12194440e-4, b, ALU.mult, ALU.add)
                    ts(o, b, 1.0 / 5040, None, ALU.mult)
                    for k in (720, 120, 24, 6, 2, 1):
                        stt(o, o, 1.0 / k, b, ALU.add, ALU.mult)
                    ts(o, o, 1.0, None, ALU.add)
                    ts(b, a, -126.0, 127.0, ALU.max, ALU.min)
                    tt(a, a, b, ALU.subtract)
                    for e_ in (b, a):
                        ts(c, e_, 127.0, 8388608.0, ALU.add, ALU.mult)
                        G.tensor_copy(pti, c)
                        pool.drain()
                        tt(o, o, pti.bitcast(fp32), ALU.mult)

                dt_, mg, th, cs, sn = col(0), col(1), col(2), col(3), col(4)
                a, b, c, d_, e_, g_, h_ = (col(i) for i in range(5, 12))
                exp(dt_, ldt, a, b, c)
                tt(d_, lre, dt_, ALU.mult)
                exp(mg, d_, a, b, c)
                tt(th, lim, dt_, ALU.mult)
                ts(a, th, 2.0 / math.pi, MAGIC, ALU.mult, ALU.add)
                ts(a, a, -MAGIC, None, ALU.add)
                parts, rest = [], math.pi / 2
                for bits in (8, 9, 10):
                    scale = 2.0 ** (bits - 1 - math.floor(math.log2(rest)))
                    v = math.floor(rest * scale) / scale
                    parts.append(v)
                    rest -= v
                parts.append(rest)
                stt(b, a, -parts[0], th, ALU.mult, ALU.add)
                for v in parts[1:]:
                    stt(b, a, -v, b, ALU.mult, ALU.add)
                tt(c, b, b, ALU.mult)
                ts(sn, c, 1.0 / 362880, None, ALU.mult)
                for k in (-5040, 120, -6):
                    stt(sn, sn, 1.0 / k, c, ALU.add, ALU.mult)
                stt(sn, sn, 1.0, b, ALU.add, ALU.mult)
                ts(cs, c, -1.0 / 3628800, None, ALU.mult)
                for k in (40320, -720, 24, -2):
                    stt(cs, cs, 1.0 / k, c, ALU.add, ALU.mult)
                ts(cs, cs, 1.0, None, ALU.add)
                ts(b, a, 0.25, MAGIC, ALU.mult, ALU.add)
                ts(b, b, -MAGIC, None, ALU.add)
                stt(a, b, -4.0, a, ALU.mult, ALU.add)
                ts(b, a, 0.0, None, ALU.is_equal)
                tt(c, a, a, ALU.mult)
                ts(c, c, 4.0, None, ALU.is_equal)
                tt(b, b, c, ALU.subtract)
                ts(c, a, 1.0, None, ALU.is_equal)
                ts(d_, a, -1.0, None, ALU.is_equal)
                tt(c, c, d_, ALU.subtract)
                tt(d_, cs, b, ALU.mult)
                tt(e_, sn, c, ALU.mult)
                tt(d_, d_, e_, ALU.subtract)
                tt(e_, sn, b, ALU.mult)
                tt(g_, cs, c, ALU.mult)
                tt(e_, e_, g_, ALU.add)
                G.tensor_copy(ph[:, 0, 0, :], d_)
                G.tensor_copy(ph[:, 0, 1, :], e_)
                G.tensor_copy(mag[:, :], mg)
                pool.drain()
                for l in range(7):
                    pr, pi_ = ph[:, l, 0, :], ph[:, l, 1, :]
                    tt(a, pr, pr, ALU.mult)
                    tt(b, pi_, pi_, ALU.mult)
                    tt(ph[:, l + 1, 0, :], a, b, ALU.subtract)
                    tt(a, pr, pi_, ALU.mult)
                    ts(ph[:, l + 1, 1, :], a, 2.0, None, ALU.mult)
                tt(a, mg, d_, ALU.mult)
                ts(a, a, -1.0, None, ALU.add)
                tt(b, mg, e_, ALU.mult)
                c = col(12)
                tt(g_, a, lre, ALU.mult)
                tt(h_, b, lim, ALU.mult)
                tt(g_, g_, h_, ALU.add)
                tt(g_, g_, c, ALU.mult)
                tt(h_, b, lre, ALU.mult)
                tt(b, a, lim, ALU.mult)
                tt(h_, h_, b, ALU.subtract)
                tt(h_, h_, c, ALU.mult)
                B = sB.rearrange("p a b t -> p (a b t)").rearrange("p (a m c) -> p a m c", a=2, m=KD)
                o = sT1.rearrange("p a b t -> p (a b t)").rearrange("p (a m c) -> p a m c", a=2, m=KD)
                w = sT2.rearrange("p a b t -> p (a b t)").rearrange("p (a m c) -> p a m c", a=2, m=KD)
                pool.wait_ge(even_loads, 48)
                fr = g_.unsqueeze(2).broadcast_to([P, KD, 32])
                fi = h_.unsqueeze(2).broadcast_to([P, KD, 32])
                tt(o[:, 0], B[:, 0], fr, ALU.mult)
                tt(w[:, 0], B[:, 1], fi, ALU.mult)
                tt(o[:, 0], o[:, 0], w[:, 0], ALU.subtract)
                tt(o[:, 1], B[:, 1], fr, ALU.mult)
                tt(w[:, 0], B[:, 0], fi, ALU.mult)
                G.tensor_tensor(o[:, 1], o[:, 1], w[:, 0], ALU.add).then_inc(bb_ready, 1)

            def phasors(k, h0, r):
                m = 4 * h0 + 2 * k
                G.tensor_copy(phst[:, :, :, :], ph[:, :, :, m:m + 2] if r is None else ph[:, :, :, ds(r * 4 + m, 2)])
                e = E[:, k]
                G.memset(e[:, 0, :, 0:1], 1.0)
                G.memset(e[:, 1, :, 0:1], 0.0)
                for l in range(8):
                    n = 1 << l
                    pool.drain()
                    c, s_ = (phst[:, l, ri, :].unsqueeze(1).unsqueeze(3).broadcast_to([P, 2, 2, n]) for ri in range(2))
                    G.tensor_tensor(g1[:, :, :, 0:n], e[:, :, :, 0:n], c, ALU.mult)
                    G.tensor_tensor(g2[:, :, :, 0:n], e[:, :, :, 0:n], s_, ALU.mult)
                    pool.drain()
                    G.tensor_tensor(e[:, 0, :, n:2 * n], g1[:, 0, :, 0:n], g2[:, 1, :, 0:n], ALU.subtract)
                    G.tensor_tensor(e[:, 1, :, n:2 * n], g1[:, 1, :, 0:n], g2[:, 0, :, 0:n], ALU.add)

            def rotate_in(k, h0, r):
                m = 4 * h0 + 2 * k
                pool.drain()
                pool.wait_ge(bu_copied, at(m + 2, 4, r))
                if m:
                    pool.wait_ge(c_done, at(m // 2, 2, r))
                G.tensor_copy(magst[:, :], mag[:, m:m + 2] if r is None else mag[:, ds(r * 4 + m, 2)])
                e = E[:, k]
                G.tensor_tensor(sT1, sB, e[:, 0:1].broadcast_to([P, 2, 2, T]), ALU.mult)
                G.tensor_tensor(sT2, sB, e[:, 1:2].broadcast_to([P, 2, 2, T]), ALU.mult)
                pool.drain()
                G.tensor_tensor(sB[:, 0], sT1[:, 0], sT2[:, 1], ALU.add)
                G.tensor_tensor(sB[:, 1], sT1[:, 1], sT2[:, 0], ALU.subtract).then_inc(w_ready, 1)

            def s5_chunk(h0, r):
                if h0:
                    pool.wait_ge(bu_done, at(4 * h0, 4, r))
                if r is None:
                    G.tensor_copy(Bst[:, :, :], BT[:, h0, :, :])
                    G.tensor_copy(Ust[:, :], U[:, h0, :]).then_inc(staged, 1)
                else:
                    G.tensor_copy(Bst[:, :, :], BT[:, ds(r + h0, 1), :, :].rearrange("p a b c -> p (a b) c"))
                    G.tensor_copy(Ust[:, :], U[:, ds(r + h0, 1), :].rearrange("p a t -> p (a t)")).then_inc(staged, 1)
                phasors(0, h0, r)
                pool.drain()
                pool.wait_ge(cst_in, at(16 * h0 + 16, 16, r))
                G.tensor_tensor(Cst[:, :, 1, :], Cst[:, :, 1, :], minus[:, 0:1].unsqueeze(2).broadcast_to([P, 4, 32]),
                                ALU.mult).then_inc(cneg_ready, 1)
                rotate_in(0, h0, r)
                phasors(1, h0, r)
                rotate_in(1, h0, r)

            G.memset(minus[:, :], -1.0)
            pool.wait_ge(small_in, 16)
            pool.wait_ge(den_ready, 1)
            s5_setup()
            pool.wait_ge(u_ready, 1)
            pool.wait_ge(bt_ready, 2)
            s5_chunk(0, None)
            with pool.Fori(0, 3) as r:
                s5_chunk(1, r)

            def feed_forward(layer, n, e0):
                for half in range(2):
                    e = e0 + half * (2 * GS + 8)
                    s0 = (2 * layer + half) * GS
                    if half == 0:
                        pool.wait_ge(conv_in, 16 * (layer + 1))
                        pool.wait_ge(rn_ready, layer + 1)

                    def convolve(r, j0):
                        s = GS * half + j0
                        if s0 + j0:
                            pool.wait_ge(hid_ready, at(s0 + j0, 1, r))
                        src = cw[:, s, :] if r is None else cw[:, ds(r + s, 1), :].rearrange("p a c -> p (a c)")
                        G.tensor_copy(cws[:, :], src).then_inc(cws_ready, 1)
                        pool.drain()
                        pool.wait_ge(bank_free, at(e + 2 * j0 + 1, 2, r))
                        G.tensor_tensor(apad[:, 0, :, 2:T + 2], apad[:, 0, :, 2:T + 2],
                                        rn[:, :].unsqueeze(1).broadcast_to([P, 2, T]), ALU.mult)
                        pool.drain()
                        w = lambda i: cws[:, 0:8].rearrange("p (t c) -> p t c", t=2)[:, :, i:i + 1].broadcast_to([P, 2, T])
                        for i in (1, 0):
                            G.tensor_tensor(ctmp[:, i, :, :], apad[:, 0, :, i:T + i], w(i), ALU.mult)
                        for t in range(2):
                            G.tensor_scalar(cvo[:, 0, t, :], apad[:, 0, t, 2:T + 2], cws[:, 4 * t + 2:4 * t + 3],
                                            cws[:, 4 * t + 3:4 * t + 4], ALU.mult, ALU.add)
                        pool.drain()
                        G.tensor_tensor(cvo[:, 0], cvo[:, 0], ctmp[:, 1], ALU.add)
                        pool.drain()
                        G.tensor_tensor(cvo[:, 0], cvo[:, 0], ctmp[:, 0], ALU.add).then_inc(cv_ready, 1)

                    if s0 == 0:
                        convolve(None, 0)
                        with pool.Fori(0, GS - 1) as r:
                            convolve(r, 1)
                    else:
                        with pool.Fori(0, GS) as r:
                            convolve(r, 0)
                sum_squares(n, e0 + 4 * GS + 8, 8 if n < 4 else 7)

            sum_squares(1, OE_E0)
            feed_forward(0, 2, F0_E0)
            sum_squares(3, OO_E0)
            feed_forward(1, 4, F1_E0)
            pool.wait_ge(rn_ready, 3)
            for j in range(FINAL_DVE, 8):
                G.tensor_tensor(H[:, 2 * j:2 * j + 2, :], XF[:, 2 * j:2 * j + 2, :], rnb, ALU.mult).then_inc(fin_pool, 1)

        @block.tensor
        def _(pe):
            mm = nc.tensor.matmul

            def tile(p, k, n, c, width=256):
                o = k * width + c
                return hi[:, p % SLOTS, o:o + P], lo[:, p % SLOTS, o:o + P]

            def project(bank, wh, wl, x, first, last):
                mm(PS[:, bank, :], wh, x, start=first, stop=False)
                return mm(PS[:, bank, 0:T], wl, x[:, 0:T], start=False, stop=last)

            def piece(p, s, r):
                pe.wait_ge(lo_ready, at(p + 1, s, r))

            def std_piece(p, i, bank, mov, s=0, r=None, nk=4, pieces=4):
                piece(p, s, r)
                for ft in range(2):
                    for k in range(nk):
                        kk = i * nk + k
                        wh, wl = tile(p, k, nk, ft * P)
                        ins = project(bank + ft, wh, wl, mov(kk), kk == 0, i == pieces - 1 and k == nk - 1)
                ins.then_inc(piece_done, 1)

            def step(p, e, mov, s=0, se=0, r=None, before=None, after=None):
                if e >= 2:
                    pe.wait_ge(bank_free, at(e - 1, se, r))
                for i in range(4):
                    if before:
                        before(i)
                    std_piece(p + i, i, pair(e), mov, s, r)
                    if after:
                        after(i)

            XSk = lambda k: XS[:, k, :]

            def norm_sum(n):
                if n:
                    pe.wait_ge(ssq_ready, n)
                else:
                    pe.wait_ge(sq_added, 4)
                mm(PS[:, 7, 0:T], ones[:, :], acc[:, 0, :], start=True, stop=False)
                ins = mm(PS[:, 7, 0:T], ones[:, :], acc[:, 1, :], start=False, stop=n < 4)
                if n == 4:
                    pe.wait_ge(last_sq, 1)
                    for t in range(2):
                        ins = mm(PS[:, 7, 0:T], ones[:, :], lot[:, t, :], start=False, stop=t == 1)
                ins.then_inc(sum_done, 1)

            def x_split(n):
                return lambda i: pe.wait_ge(xl_ready, 8 * n + 2 * i + 2)

            pe.wait_ge(ones_set, 1)
            step(0, 0, XSk, before=x_split(0), after=lambda i: norm_sum(0) if i == 3 else None)
            step(4, 1, XSk)
            pe.wait_ge(small_in, 32)
            pe.wait_ge(bank_free, 1)
            for t in range(2):
                ins = mm(PS[:, 7, T + t:T + t + 1], rn[:, t * P:(t + 1) * P], ident[:, 0:1], start=True, stop=True)
            ins.then_inc(rt_done, 1)

            def b_transposed():
                pe.wait_ge(bb_ready, 1)
                pe.wait_ge(rt_ready, 1)
                ob = sT1.rearrange("p a b t -> p (a b t)").rearrange("p (a m) -> p a m", a=2)
                for k in range(KR):
                    for ri in range(2):
                        i = 2 * k + ri
                        ins = pe.transpose(PS[:, 6 + i // 4, (i % 4) * P:(i % 4 + 1) * P], ob[:, ri, k * P:(k + 1) * P],
                                           ident[:, :])
                ins.then_inc(bt_psum, 8)

            def even_head(r, h0, s5, glu=False):
                p0, e0 = 8 + 16 * h0, 2 + 4 * h0
                H_ = lambda c, s: at(c + s * h0, s, r)
                S_ = lambda c, s: at(c + s * (h0 - 1), s, r)

                def b_u(m):
                    if m == 0:
                        pe.wait_ge(staged, S_(1, 1))
                    if h0 - 1 + m > 0:
                        pe.wait_ge(bu_copied, S_(m, 4))
                    for ri in range(2):
                        ins = mm(PS[:, 7, ri * T:(ri + 1) * T], Bst[32 * m:32 * m + 32, ri, :], Ust[32 * m:32 * m + 32, :],
                                 start=True, stop=True)
                    ins.then_inc(bu_done, 1)

                def c_x(k):
                    pe.wait_ge(z_ready, S_(k + 1, 2))
                    if k == 0:
                        pe.wait_ge(cneg_ready, S_(1, 1))
                        if h0 > 1:
                            pe.wait_ge(y5_ready, S_(0, 1))
                    for m in range(2):
                        q = 2 * k + m
                        for ri in range(2):
                            ins = mm(PS[32 * q:32 * q + 32, 6, 0:T], Cst[:, q, ri, :], sT1[:, ri, m, :],
                                     start=ri == 0, stop=ri == 1)
                    ins.then_inc(c_done, 1)

                def after_k(i):
                    if s5 and i == 1:
                        b_u(0)

                def after_q(t):
                    if s5 and t in (0, 2):
                        b_u(1 + t // 2)
                    if glu:
                        pe.wait_ge(ge_ready, 1)
                        pe.wait_ge(gluw_in, 16)
                        for k in range(KR):
                            ins = mm(PS[:, 6 + t // 2, (t % 2) * T:(t % 2 + 1) * T], gluw[:, k, t * P:(t + 1) * P], U[:, k, :],
                                     start=k == 0, stop=k == KR - 1)
                        ins.then_inc(glu_done, 1)

                step(p0, e0, XSk, 16, 4, r, after=after_k)
                step(p0 + 4, e0 + 1, XSk, 16, 4, r, after=after_q)
                pe.wait_ge(bank_free, at(e0 + 1, 4, r))
                b = pair(e0 + 2)
                for i in range(4):
                    p = p0 + 8 + i
                    piece(p, 16, r)
                    for tt in range(2):
                        for k in range(4):
                            kk = 4 * i + k
                            xh = XS[:, kk, tt * P:(tt + 1) * P]
                            xl = XS[:, kk, T + tt * P:T + (tt + 1) * P]
                            wh, wl = hi[:, p % SLOTS, k * T:(k + 1) * T], lo[:, p % SLOTS, k * T:(k + 1) * T]
                            mm(PS[:, b + tt, 0:T], xh, wh, start=kk == 0, stop=False)
                            mm(PS[:, b + tt, 0:T], xh, wl, start=False, stop=False)
                            ins = mm(PS[:, b + tt, 0:T], xl, wh, start=False, stop=kk == KD - 1)
                    ins.then_inc(piece_done, 1)
                    if s5:
                        if i == 1:
                            c_x(0)
                            b_u(3)
                pe.wait_ge(kq_ready, H_(2, 2))
                if h0:
                    pe.wait_ge(ovar_ready, H_(0, 1))
                for k in range(2):
                    mm(PS[:, 4, 0:T], KRo[:, k, 0:P], QRo[:, k, :], start=k == 0, stop=k == 1)
                for k in range(2):
                    ins = mm(PS[:, 4, T:T + P], KRo[:, k, P:T], QRo[:, k, P:T], start=k == 0, stop=k == 1)
                ins.then_inc(s_done, 1)

                def after_g(i):
                    if i == 1:
                        pe.wait_ge(pm_ready, H_(1, 1))
                        pe.wait_ge(lo_copied, at(e0 + 3, 4, r))
                        pe.wait_ge(bank_free, at(e0 + 3, 4, r))
                        if h0:
                            pe.wait_ge(yt_ready, H_(0, 1))
                        for t in range(2):
                            mm(PS[:, 5, t * T:(t + 1) * T], Vr[:, 0, t * P:(t + 1) * P], Pm[:, 0:T], start=True, stop=False)
                            ins = mm(PS[:, 5, t * T + P:(t + 1) * T], Vr[:, 1, t * P:(t + 1) * P], Pm[:, T:T + P],
                                     start=False, stop=True)
                        ins.then_inc(o_done, 1)
                    if i == 3:
                        pe.wait_ge(osq_ready, H_(1, 1))
                        for t in range(2):
                            ins = mm(PS[:, 4, 0:T], ones[:, :], sq[:, t, :], start=t == 0, stop=t == 1)
                        ins.then_inc(osum_done, 1)
                        if s5:
                            c_x(1)
                    if i == 2 and h0 == 0:
                        b_transposed()

                step(p0 + 12, e0 + 3, XSk, 16, 4, r, after=after_g)

            even_head(None, 0, False)
            even_head(None, 1, True)
            with pe.Fori(0, 3) as r:
                even_head(r, 2, True)
            even_head(None, 5, False, True)

            YEk = lambda k: Y5[:, k, :] if k < KR else YE[:, k - KR, :]
            YOk = lambda k: YO[:, k, :]

            def out_projection(p0, e0, mov, before):
                step(p0, e0, mov, before=before)
                step(p0 + 4, e0 + 1, mov)
                with pe.Fori(0, 3) as r:
                    for i in range(2, 4):
                        step(p0 + 4 * i, e0 + i, mov, 8, 2, r)

            def feed_forward(layer, n, p0, e0):
                for half in range(2):
                    p = p0 + half * (UPP + DNP)
                    e = e0 + half * (2 * GS + 8)
                    s0 = (2 * layer + half) * GS
                    if half == 0:
                        step(p, e, XSk, before=x_split(n), after=lambda i: norm_sum(n) if i == 2 else None)
                    else:
                        step(p, e, XSk)
                    step(p + 4, e + 1, XSk)
                    with pe.Fori(0, GS // 2) as r:
                        for j in range(4):
                            step(p + 8 + 4 * j, e + 2 + j, XSk, 16, 4, r)
                    q, ed = p + UPP, e + 2 * GS

                    def down(i0, r):
                        pe.wait_ge(bank_free, at(ed + i0 - 1, 2, r))
                        for i in range(8):
                            pc = q + 8 * i0 + i
                            u, part = i // 2, i % 2
                            piece(pc, 16, r)
                            if r is None and i0 == 0 and u in (0, 2):
                                pe.wait_ge(hl_ready, s0 + ((u // 2) * GS + (6, GS)[part] + 1) // 2)
                            ft = u % 2
                            for k in range((6, 5)[part]):
                                kk = (u // 2) * GS + part * 6 + k
                                ins = project(pair(ed + i0) + ft, hi[:, pc % SLOTS, k * P:(k + 1) * P],
                                              lo[:, pc % SLOTS, k * P:(k + 1) * P], YF[:, kk, :], kk == 0, kk == GK - 1)
                            ins.then_inc(piece_done, 1)

                    down(0, None)
                    down(1, None)
                    with pe.Fori(0, 3) as r:
                        down(2, r)
                        down(3, r)

            def even_inputs(i):
                if i == 0:
                    pe.wait_ge(glu_lo, 1)
                if i in (1, 3):
                    pe.wait_ge(yl_ready, RH - (i == 1))

            out_projection(OE_P0, OE_E0, YEk, even_inputs)
            feed_forward(0, 1, F0_P0, F0_E0)

            q = MD_P0

            def c_squares(j):
                pe.wait_ge(csq_ready, j + 1)
                for t in range(2):
                    ins = mm(PS[:, 6 + j // 2, 0:T], ones[:, :], txn[:, j % 2, t, :], start=j % 2 == 0 and t == 0,
                             stop=j % 2 == 1 and t == 1)
                ins.then_inc(csum_done, 1)

            for i in range(2):
                pc = q + i
                pe.wait_ge(xl_ready, 8 * 2 + 4 * i + 4)
                piece(pc, 0, None)
                if i == 0:
                    pe.wait_ge(bank_free, MD_E0 - 1)
                for k in range(8):
                    kk = 8 * i + k
                    ins = project(pair(MD_E0), hi[:, pc % SLOTS, k * P:(k + 1) * P], lo[:, pc % SLOTS, k * P:(k + 1) * P],
                                  XS[:, kk, :], kk == 0, kk == KD - 1)
                ins.then_inc(piece_done, 1)

            def swap(x, bank, ready, count):
                pe.wait_ge(ready, count)
                mm(PS[:, bank, 0:T], swp[:, :], x, start=True, stop=True).then_inc(sw_done, 1)

            step(q + 2, MD_E0 + 1, XSk, after=lambda i: norm_sum(2) if i == 0 else None)

            def key_sums(i):
                if i == 1:
                    pe.wait_ge(odd_loads, 64)
                    swap(KX[:, :], 5, kx_ready, 1)
                if i == 2:
                    c_squares(0)

            step(q + 6, MD_E0 + 2, XSk, after=key_sums)
            step(q + 10, MD_E0 + 3, XSk, after=lambda i: c_squares(1) if i == 2 else None)
            step(q + 14, MD_E0 + 4, XSk, after=lambda i: c_squares(2) if i == 2 else None)

            def queries(p0, c0, r):
                if c0:
                    pe.wait_ge(lo_ready, at(p0 + 2, 8, r))
                    pe.wait_ge(qr_ready, at(c0 + 1, 2, r))
                else:
                    pe.wait_ge(lo_ready, p0 + 4)
                    pe.wait_ge(bank_free, MD_E0 + 5)
                    pe.wait_ge(cl_ready, 4)
                for b in range(3):
                    for k in range(KR):
                        pc = p0 + (2 if c0 == 0 else 0) + k // 2
                        o = (k % 2) * 3 * P + b * P
                        ins = project(b, hi[:, pc % SLOTS, o:o + P], lo[:, pc % SLOTS, o:o + P], CS[:, 4 + k, :], k == 0, k == KR - 1)
                ins.then_inc(piece_done, 2)

            def keys_values(p0, c0, r):
                if c0 == 0:
                    pe.wait_ge(lo_ready, p0 + 2)
                    pe.wait_ge(cl_ready, 2)
                    pe.wait_ge(qr_ready, 1)
                    pe.wait_ge(bank_free, MD_E0 + 4)
                else:
                    pe.wait_ge(lo_ready, at(p0 + 4, 8, r))
                    pe.wait_ge(v2_ready, at(c0, 2, r))
                    pe.wait_ge(kb_free, at(c0, 2, r))
                w = lambda x, k: x[:, (p0 + (2 if c0 else 0) + k // 2) % SLOTS, (k % 2) * 512:(k % 2 + 1) * 512].rearrange("p (h c) -> p h c", h=2)
                for h in range(2):
                    for k in range(KR):
                        project(3 + h, w(hi, k)[:, h, 0:P], w(lo, k)[:, h, 0:P], CS[:, k, :], k == 0, k == KR - 1)
                for tt in range(2):
                    o = PS[:, 5, tt * T:(tt + 1) * T]
                    if c0 == 0 and tt == 1:
                        c_squares(3)
                    for k in range(KR):
                        xh, xl = CS[:, k, tt * P:(tt + 1) * P], CS[:, k, T + tt * P:T + (tt + 1) * P]
                        mm(o, xh, w(hi, k)[:, :, P:2 * P], start=k == 0, stop=False)
                        mm(o, xh, w(lo, k)[:, :, P:2 * P], start=False, stop=False)
                        ins = mm(o, xl, w(hi, k)[:, :, P:2 * P], start=False, stop=k == KR - 1)
                ins.then_inc(piece_done, 2)

            def scores(c0, r):
                pe.wait_ge(kb_free, at(c0 + 1, 2, r))
                pe.wait_ge(qr_ready, at(c0 + 2, 2, r))
                for h in range(2):
                    if c0:
                        pe.wait_ge(pt_ready, at(2 * c0 + h - 1, 4, r))
                    R = slice(MR * h, MR * h + MR)
                    for qt in range(2):
                        o = PS[:, 6 + h, 0:P] if qt == 0 else PS[:, 6 + h, P:3 * P]
                        n = P * (qt + 1)
                        mm(o, QN[:, h, qt * P:(qt + 1) * P], KN[:, h, 0:n], start=True, stop=False)
                        ins = mm(o, QRp[R, qt * P:(qt + 1) * P], KRp[R, 0:n], start=False, stop=True)
                    ins.then_inc(sc_done, 1)

            def attend(c0, r, kb, between=None):
                for h in range(2):
                    pe.wait_ge(pn_ready, at(2 * c0 + h + 1, 4, r))
                    for i in range(3):
                        ins = pe.transpose(PS[:, 6 + h, i * P:(i + 1) * P], Sc[:, h, i * P:(i + 1) * P], ident[:, :])
                    ins.then_inc(pt_done, 1)
                if between:
                    between()
                pe.wait_ge(v2_ready, at(c0 + 1, 2, r))
                pe.wait_ge(kb_free, at(kb, 2, r))
                for h in range(2):
                    pe.wait_ge(pt_ready, at(2 * c0 + h + 1, 4, r))
                    mm(PS[:, 3, h * T:(h + 1) * T], V2[:, 0, h * P:(h + 1) * P], PT[:, h, 0:T], start=True, stop=False)
                    ins = mm(PS[:, 3, h * T + P:(h + 1) * T], V2[:, 1, h * P:(h + 1) * P], PT[:, h, T:3 * P],
                             start=False, stop=True)
                ins.then_inc(at_done, 1)

            def pair_body(r, c0):
                p0 = MP_P0 + 4 * c0
                queries(p0, c0, r)
                scores(c0 - 1, r)
                keys_values(p0, c0, r)
                attend(c0 - 1, r, c0 + 1, lambda: swap(QX[:, :], 2, qa_free, at(c0 + 1, 2, r)))

            keys_values(MP_P0, 0, None)
            queries(MP_P0, 0, None)
            swap(QX[:, :], 2, qa_free, 1)
            with pe.Fori(0, 3) as r:
                pair_body(r, 1)
                pair_body(r, 2)
            pair_body(None, 7)
            scores(7, None)

            def odd_inputs(i):
                if i == 0:
                    pe.wait_ge(al_ready, 6)
                if i == 2:
                    attend(7, None, 8)
                if i == 3:
                    pe.wait_ge(al_ready, 8)
            out_projection(OO_P0, OO_E0, YOk, odd_inputs)
            feed_forward(1, 3, F1_P0, F1_E0)
            norm_sum(4)


def tables():
    t = np.arange(T, dtype=np.float32)

    def rope(dim):
        inv = np.power(np.float32(10000.0), -np.arange(0, dim, 2, dtype=np.float32) / np.float32(dim))
        ang = (t[None, :] * inv[:, None]).astype(np.float32)
        return np.cos(ang).astype(np.float32), np.sin(ang).astype(np.float32)

    cosR, sinR = rope(RD)
    c, s = rope(MR)
    j, i = np.arange(P)[:, None], np.arange(T)[None, :]
    lg = np.log(1.0 - 2.0 ** (-5.0 - np.arange(RH, dtype=np.float64)))
    dec = np.where(i >= j, np.exp(np.maximum(i - j, 0)[None] * lg[:, None, None]), 0.0) * RD ** -0.5
    q = np.arange(P)[:, None]
    tri = np.where(q >= np.arange(P)[None, :], 0.0, -1e30)
    caus = np.concatenate([tri, np.zeros((P, P)), tri], axis=1)
    swp = np.zeros((P, P))
    for m in range(P):
        swp[(m // MR) * MR + (m + MR // 2) % MR, m] = 1.0
    f = lambda a: np.ascontiguousarray(a, dtype=np.float32)
    return {"cosR": f(cosR), "sinR": f(sinR), "mcos": f(np.concatenate([c, c, c, c])),
            "msin": f(np.concatenate([-s, s, -s, s])), "dec": f(dec), "caus": f(caus), "swp": f(swp),
            "ident": f(np.eye(P))}


def kernel(**inputs):
    from concourse import bacc
    from concourse.bass_utils import run_bass_kernel_spmd

    a = {k: np.asarray(v) for k, v in inputs.items()}
    ct = np.ascontiguousarray

    def columns(v):
        return v.reshape(-1, P).T

    def units(w, k, n):
        rows, cols = w.shape
        w = w.reshape(rows // (k * P), k, P, cols // n, n)
        return ct(w.transpose(3, 0, 2, 1, 4).reshape(-1, P, k * n))

    wi = a["w_in_even"][0]
    sec = lambda i, h: wi[:, S5W + i * RH * RD + h * RD:S5W + i * RH * RD + (h + 1) * RD]
    w_in = np.concatenate([wi[:, :S5W]] + [sec(i, h) for h in range(RH) for i in (1, 0, 2, 3)], axis=1)
    dn = a["mla_w_down"][0]
    kr = dn[:, 2 * RANK:]
    uq = a["mla_w_uq"][0].reshape(RANK, MH // 2, 2, MN + MR)
    w_uq = np.concatenate([uq[..., :MN].reshape(RANK, MH // 2, -1), uq[..., MN:].reshape(RANK, MH // 2, -1)],
                          axis=2).reshape(RANK, -1)
    data = {
        "x": ct(a["x"][0].T.reshape(KD, P, T).transpose(1, 0, 2)),
        "w_in": units(w_in, 8, 256),
        "w_oe": units(a["w_out_even"][0], 8, 256),
        "w_oo": units(a["w_out_odd"][0], 8, 256),
        "mla_dn": np.concatenate([units(np.concatenate([kr, kr], axis=1), 16, P),
                                  units(np.concatenate([dn[:, RANK:2 * RANK], dn[:, :RANK]], axis=1), 8, 256)]),
        "w_uq": units(w_uq, 4, 2 * (MN + MR)),
        "w_ukv": units(a["mla_w_ukv"][0], 4, 2 * (MN + MV)),
    }
    up, down = [], []
    for l in range(2):
        w = a["ffn_w_up"][l].reshape(D, 2, FS, 256)
        up.append(units(ct(w.transpose(0, 2, 1, 3)).reshape(D, 2 * DFF), 8, 256))
        w = a["ffn_w_down"][l].reshape(2, 2, GS, P, 8, 2, P)
        down.append(w.transpose(0, 4, 1, 5, 3, 2, 6).reshape(-1, P, GS * P))
    data["ffn_up"], data["ffn_dn"] = np.concatenate(up), ct(np.concatenate(down))
    cwt = np.concatenate([a["ffn_conv_w"], a["ffn_conv_b"][:, None, :]], axis=1)
    data["conv"] = ct(cwt.reshape(2, 4, 2, FS, 2, P).transpose(0, 5, 3, 2, 4, 1).reshape(2, P, FS, 16))
    ldt = np.repeat(a["s5_log_dt"][0][:, None], S5P, axis=1).reshape(-1)
    data["vec"] = ct(np.concatenate([columns(v.reshape(-1)) for v in (
        a["ln_mix_even"], a["ln_mix_odd"], a["ln_ffn"], a["ln_final"], a["ret_norm"], a["s5_d"], a["s5_glu_b"],
        a["mla_q_norm"], a["mla_kv_norm"], a["s5_lambda_re"], a["s5_lambda_im"], ldt)], axis=1))
    b = np.zeros((P, 2, KD, 2, S5H), np.float32)
    c = np.zeros((KR, P, 4, 2, 2, S5H), np.float32)
    for ri, n in enumerate(("re", "im")):
        bg = a["s5_b_" + n][0].reshape(KD, 2, S5P, S5H)
        cg = a["s5_c_" + n][0].reshape(KR, 4, 2, S5H, S5P)
        for g in range(2):
            b[g * S5P:(g + 1) * S5P, ri, :, g, :] = bg[:, g].transpose(1, 0, 2)
            c[:, g * S5P:(g + 1) * S5P, :, ri, g, :] = cg[:, :, g].transpose(0, 3, 1, 2)
    data["s5b"], data["s5c"] = b.reshape(P, -1), c.reshape(KR, P, -1)
    data["gluw"] = ct(a["s5_glu_w"][0].reshape(KR, P, S5W).transpose(1, 0, 2))
    data.update(tables())

    nc = bacc.Bacc("TRN2", target_bir_lowering=False, num_devices=1)
    A = {k: nc.dram_tensor("in_" + k, v.shape, mybir.dt.from_np(v.dtype), kind="ExternalInput").ap()
         for k, v in data.items()}
    out = nc.dram_tensor("out", (P, KD, T), mybir.dt.float32, kind="ExternalOutput").ap()
    build(nc, A, out)
    r = run_bass_kernel_spmd(nc, [{"in_" + k: v for k, v in data.items()}], core_ids=[0])
    y = r.results[0]["out"]
    return ct(y.transpose(2, 1, 0).reshape(1, T, D))
```
